# Optimizing a Trainium2 kernel written in Bass

```python
import jax, jax.numpy as jnp
from jax import lax
import numpy as np

D_MODEL = 2048
BATCH = 1
SEQ = 256
DEPTH = 2

A_HEADS = 16
A_KV_HEADS = 2
A_HEAD_DIM = 64
WINDOW = 128
B_HEADS = 8
B_HEAD_DIM = 128
CONV_K = 4
DN_CHUNK = 64
C_WIDTH = D_MODEL
C_GROUPS = 8
C_CHUNK = 128
C_GROUP_DIM = C_WIDTH // C_GROUPS
D_FF = -(-8 * D_MODEL // (3 * 256)) * 256
EPS = 1e-6

A_Q = A_HEADS * A_HEAD_DIM
A_KV = A_KV_HEADS * A_HEAD_DIM
B_W = B_HEADS * B_HEAD_DIM
EVEN_IN = A_Q + 2 * A_KV + 4 * B_W + 2 * B_HEADS
MIX_OUT = A_Q + B_W
EVEN_SPLITS = [int(s) for s in np.cumsum([A_Q, A_KV, A_KV, 3 * B_W, B_W, B_HEADS])]


def rms_norm(x, g):
    xf = x.astype(jnp.float32)
    y = xf * lax.rsqrt(jnp.mean(xf * xf, axis=-1, keepdims=True) + EPS)
    return (y * g.astype(jnp.float32)).astype(x.dtype)

def layer_norm(x, g, b):
    xf = x.astype(jnp.float32)
    mu = jnp.mean(xf, axis=-1, keepdims=True)
    var = jnp.mean(jnp.square(xf - mu), axis=-1, keepdims=True)
    y = (xf - mu) * lax.rsqrt(var + EPS)
    return (y * g.astype(jnp.float32) + b.astype(jnp.float32)).astype(x.dtype)

def l2_norm(x):
    return x * lax.rsqrt(jnp.sum(x * x, axis=-1, keepdims=True) + EPS)

def sliding_window_attention(q, k, v, sinks):
    b, t, hq, dh = q.shape
    hkv = k.shape[2]
    grp = hq // hkv
    nb = t // WINDOW
    qb = q.astype(jnp.float32).reshape(b, nb, WINDOW, hkv, grp, dh)

    def with_prev(x):
        xb = x.astype(jnp.float32).reshape(b, nb, WINDOW, hkv, dh)
        prev = jnp.pad(xb, ((0, 0), (1, 0), (0, 0), (0, 0), (0, 0)))[:, :-1]
        return jnp.concatenate([prev, xb], axis=2)

    kb, vb = with_prev(k), with_prev(v)
    s = jnp.einsum('bnqhgd,bnkhd->bnhgqk', qb, kb) * (dh ** -0.5)
    r = jnp.arange(WINDOW)[:, None]
    c = jnp.arange(2 * WINDOW)[None, :]
    rel = r + WINDOW - c
    blk = jnp.arange(nb)[:, None, None]
    valid = (rel >= 0) & (rel < WINDOW) & (blk * WINDOW - WINDOW + c >= 0)
    s = jnp.where(valid[None, :, None, None], s, -jnp.inf)
    sink = sinks.astype(jnp.float32).reshape(1, 1, hkv, grp, 1, 1)
    m = jnp.maximum(jnp.max(s, axis=-1, keepdims=True), sink)
    p = jnp.exp(s - m)
    denom = jnp.sum(p, axis=-1, keepdims=True) + jnp.exp(sink - m)
    o = jnp.einsum('bnhgqk,bnkhd->bnqhgd', p / denom, vb)
    return o.reshape(b, t, hq * dh).astype(q.dtype)

def causal_conv_silu(x, w):
    kk, ch = w.shape
    y = lax.conv_general_dilated(
        x, w[:, None, :].astype(x.dtype), window_strides=(1,),
        padding=((kk - 1, 0),), dimension_numbers=('NWC', 'WIO', 'NWC'),
        feature_group_count=ch)
    return jax.nn.silu(y)

def gated_delta_rule(q, k, v, beta, g):
    b, t, h, dk = q.shape
    dv = v.shape[-1]
    c = DN_CHUNK
    n = t // c

    def chunks(x):
        x = jnp.moveaxis(x, 2, 1)
        return x.reshape(b, h, n, c, *x.shape[3:])

    q, k, v, beta, g = (chunks(a) for a in (q, k, v, beta, g))
    gam = jnp.cumsum(g, axis=-1)
    idx = jnp.arange(c)
    incl = idx[:, None] >= idx[None, :]
    strict = idx[:, None] > idx[None, :]
    decay = jnp.exp(jnp.where(incl, gam[..., :, None] - gam[..., None, :], -jnp.inf))
    kk = jnp.einsum('bhnid,bhnjd->bhnij', k, k)
    a_mat = jnp.where(strict, beta[..., :, None] * kk * decay, 0.0) + jnp.eye(c, dtype=q.dtype)
    rhs = jnp.concatenate([v * beta[..., None], k * (beta * jnp.exp(gam))[..., None]], axis=-1)
    sol = lax.linalg.triangular_solve(a_mat, rhs, left_side=True, lower=True, unit_diagonal=True)
    u, w = sol[..., :dv], sol[..., dv:]
    qk = jnp.einsum('bhnid,bhnjd->bhnij', q, k) * decay
    q_dec = q * jnp.exp(gam)[..., None]
    k_dec = k * jnp.exp(gam[..., -1:] - gam)[..., None]
    g_last = jnp.exp(gam[..., -1])

    def step(state, xs):
        qd, kd, wc, uc, qkc, gl = xs
        v_new = uc - jnp.einsum('bhck,bhkv->bhcv', wc, state)
        o = jnp.einsum('bhck,bhkv->bhcv', qd, state) + jnp.einsum('bhij,bhjv->bhiv', qkc, v_new)
        state = state * gl[..., None, None] + jnp.einsum('bhck,bhcv->bhkv', kd, v_new)
        return state, o

    xs = tuple(jnp.moveaxis(a, 2, 0) for a in (q_dec, k_dec, w, u, qk, g_last))
    s0 = jnp.zeros((b, h, dk, dv), q.dtype)
    _, o = lax.scan(step, s0, xs)
    return jnp.transpose(o, (1, 0, 3, 2, 4)).reshape(b, t, h, dv)

def even_mixer(hn, w_in, conv_w, a_log, dt_bias, sinks, onorm, w_out):
    b, t, _ = hn.shape
    proj = hn @ w_in
    qa, ka, va, qkv_b, z, beta_raw, a_raw = jnp.split(proj, EVEN_SPLITS, axis=-1)
    out_a = sliding_window_attention(
        qa.reshape(b, t, A_HEADS, A_HEAD_DIM),
        ka.reshape(b, t, A_KV_HEADS, A_HEAD_DIM),
        va.reshape(b, t, A_KV_HEADS, A_HEAD_DIM), sinks)
    qkv_b = causal_conv_silu(qkv_b, conv_w).astype(jnp.float32)
    qb, kb, vb = jnp.split(qkv_b, 3, axis=-1)
    qb = l2_norm(qb.reshape(b, t, B_HEADS, B_HEAD_DIM)) * (B_HEAD_DIM ** -0.5)
    kb = l2_norm(kb.reshape(b, t, B_HEADS, B_HEAD_DIM))
    vb = vb.reshape(b, t, B_HEADS, B_HEAD_DIM)
    beta = jax.nn.sigmoid(beta_raw.astype(jnp.float32))
    g = -jnp.exp(a_log.astype(jnp.float32)) * jax.nn.softplus(
        a_raw.astype(jnp.float32) + dt_bias.astype(jnp.float32))
    o = gated_delta_rule(qb, kb, vb, beta, g)
    o = o * lax.rsqrt(jnp.mean(o * o, axis=-1, keepdims=True) + EPS) * onorm.astype(jnp.float32)
    o = o * jax.nn.silu(z.astype(jnp.float32).reshape(b, t, B_HEADS, B_HEAD_DIM))
    out_b = o.reshape(b, t, B_W).astype(hn.dtype)
    return jnp.concatenate([out_a, out_b], axis=-1) @ w_out

def odd_mixer(hn, w_in, ln_g, ln_b, w_s, b_s, w_out):
    b, t, _ = hn.shape
    zz = jax.nn.gelu(hn @ w_in, approximate=False)
    u, v = jnp.split(zz, 2, axis=-1)
    v = layer_norm(v, ln_g, ln_b)
    nb = t // C_CHUNK
    vb = v.reshape(b, nb, C_CHUNK, C_GROUPS, C_GROUP_DIM)
    ws = jnp.tril(w_s)
    mixed = jnp.einsum('gts,bnsgc->bntgc', ws, vb) + b_s.T[None, None, :, :, None]
    return (u * mixed.reshape(b, t, C_WIDTH)) @ w_out

def swiglu(hn, w_gate, w_up, w_down):
    return (jax.nn.silu(hn @ w_gate) * (hn @ w_up)) @ w_down

def first_inputs(seed: int = 0) -> dict:
    key = jax.random.key(seed)
    ks = jax.random.split(key, 22)
    ne, no = (DEPTH + 1) // 2, DEPTH // 2
    f32 = jnp.float32

    def nrm(k, shape, scale):
        return jax.random.normal(k, shape, f32) * scale

    def gain(k, shape):
        return 1.0 + 0.05 * jax.random.normal(k, shape, f32)

    return {
        "x": nrm(ks[0], (BATCH, SEQ, D_MODEL), 1.0),
        "even_norm": gain(ks[1], (ne, D_MODEL)),
        "even_w_in": nrm(ks[2], (ne, D_MODEL, EVEN_IN), D_MODEL ** -0.5),
        "even_conv": nrm(ks[3], (ne, CONV_K, 3 * B_W), CONV_K ** -0.5),
        "even_a_log": jnp.log(jax.random.uniform(ks[4], (ne, B_HEADS), f32, 1.0, 16.0)),
        "even_dt_bias": nrm(ks[5], (ne, B_HEADS), 0.1),
        "even_sinks": nrm(ks[6], (ne, A_HEADS), 1.0),
        "even_onorm": gain(ks[7], (ne, B_HEAD_DIM)),
        "even_w_out": nrm(ks[8], (ne, MIX_OUT, D_MODEL), MIX_OUT ** -0.5),
        "odd_norm": gain(ks[9], (no, D_MODEL)),
        "odd_w_in": nrm(ks[10], (no, D_MODEL, 2 * C_WIDTH), D_MODEL ** -0.5),
        "odd_ln_g": gain(ks[11], (no, C_WIDTH)),
        "odd_ln_b": nrm(ks[12], (no, C_WIDTH), 0.02),
        "odd_w_s": nrm(ks[13], (no, C_GROUPS, C_CHUNK, C_CHUNK), C_CHUNK ** -0.5),
        "odd_b_s": 1.0 + nrm(ks[14], (no, C_GROUPS, C_CHUNK), 0.1),
        "odd_w_out": nrm(ks[15], (no, C_WIDTH, D_MODEL), C_WIDTH ** -0.5),
        "ffn_norm": gain(ks[16], (DEPTH, D_MODEL)),
        "ffn_w_gate": nrm(ks[17], (DEPTH, D_MODEL, D_FF), D_MODEL ** -0.5),
        "ffn_w_up": nrm(ks[18], (DEPTH, D_MODEL, D_FF), D_MODEL ** -0.5),
        "ffn_w_down": nrm(ks[19], (DEPTH, D_FF, D_MODEL), D_FF ** -0.5),
        "final_norm": gain(ks[20], (D_MODEL,)),
    }

def first_block(x, even_norm, even_w_in, even_conv, even_a_log, even_dt_bias, even_sinks,
              even_onorm, even_w_out, odd_norm, odd_w_in, odd_ln_g, odd_ln_b, odd_w_s,
              odd_b_s, odd_w_out, ffn_norm, ffn_w_gate, ffn_w_up, ffn_w_down, final_norm):
    h = x
    for i in range(DEPTH):
        j = i // 2
        if i % 2 == 0:
            h = h + even_mixer(rms_norm(h, even_norm[j]), even_w_in[j], even_conv[j],
                               even_a_log[j], even_dt_bias[j], even_sinks[j],
                               even_onorm[j], even_w_out[j])
        else:
            h = h + odd_mixer(rms_norm(h, odd_norm[j]), odd_w_in[j], odd_ln_g[j],
                              odd_ln_b[j], odd_w_s[j], odd_b_s[j], odd_w_out[j])
        h = h + swiglu(rms_norm(h, ffn_norm[i]), ffn_w_gate[i], ffn_w_up[i], ffn_w_down[i])
    return rms_norm(h, final_norm)


DEPTH_2 = 1

MIX_W = D_MODEL
ATT_W = MIX_W // 2
HEAD_DIM = 128
N_ATT_HEADS = ATT_W // HEAD_DIM
CONV_W = MIX_W // 4
CONV_TAPS = 3
POOL_W = MIX_W - ATT_W - CONV_W
POOL_WINDOWS = (2, 4, 8, 16)
POOL_GROUP = POOL_W // len(POOL_WINDOWS)
Q_BLOCK = 128
LN_EPS = 1e-5
DEEPNORM_ALPHA = (2 * DEPTH_2) ** 0.25
DEEPNORM_BETA = (8 * DEPTH_2) ** -0.25

IN_WIDTHS = (ATT_W, ATT_W, ATT_W, ATT_W, N_ATT_HEADS,
             CONV_W, CONV_W, CONV_W, CONV_W, POOL_W, POOL_W)
IN_W = sum(IN_WIDTHS)
IN_SPLITS = tuple(sum(IN_WIDTHS[:i + 1]) for i in range(len(IN_WIDTHS) - 1))


def layer_norm_2(x, g, b):
    x32 = x.astype(jnp.float32)
    mu = jnp.mean(x32, axis=-1, keepdims=True)
    var = jnp.mean(jnp.square(x32 - mu), axis=-1, keepdims=True)
    return ((x32 - mu) * lax.rsqrt(var + LN_EPS) * g + b).astype(x.dtype)

def forgetting_attention(q, k, v, fg_logit, b_f):
    b, s, h, dh = q.shape
    nb = s // Q_BLOCK
    log_f = jax.nn.log_sigmoid(fg_logit.astype(jnp.float32) + b_f.astype(jnp.float32))
    cum = jnp.cumsum(log_f, axis=1)
    cum_k = jnp.transpose(cum, (0, 2, 1))
    q_blocks = q.reshape(b, nb, Q_BLOCK, h, dh).transpose(1, 0, 2, 3, 4)
    c_blocks = cum.reshape(b, nb, Q_BLOCK, h).transpose(1, 0, 3, 2)
    k_pos = jnp.arange(s)
    scale = HEAD_DIM ** -0.5

    def block(args):
        qb, cb, i = args
        logits = jnp.einsum('bqhd,bkhd->bhqk', qb, k).astype(jnp.float32) * scale
        logits = logits + cb[..., None] - cum_k[:, :, None, :]
        q_pos = i * Q_BLOCK + jnp.arange(Q_BLOCK)
        causal = k_pos[None, :] <= q_pos[:, None]
        logits = jnp.where(causal, logits, -jnp.inf)
        p = jax.nn.softmax(logits, axis=-1).astype(v.dtype)
        return jnp.einsum('bhqk,bkhd->bqhd', p, v)

    out = lax.map(block, (q_blocks, c_blocks, jnp.arange(nb)))
    return out.transpose(1, 0, 2, 3, 4).reshape(b, s, h * dh)

def short_conv_mixer(gate_b, gate_c, h, conv_w):
    s = h.shape[1]
    u = gate_c * h
    up = jnp.pad(u, ((0, 0), (CONV_TAPS - 1, 0), (0, 0)))
    y = conv_w[0] * up[:, 0:s]
    for j in range(1, CONV_TAPS):
        y = y + conv_w[j] * up[:, j:j + s]
    return gate_b * y

def multiscale_pool_mixer(u, pool_w, pool_scale):
    s = u.shape[1]
    u32 = u.astype(jnp.float32)
    cs = jnp.pad(jnp.cumsum(u32, axis=1), ((0, 0), (1, 0), (0, 0)))
    t1 = jnp.arange(1, s + 1, dtype=jnp.float32)
    outs = []
    for g, w in enumerate(POOL_WINDOWS):
        sl = slice(g * POOL_GROUP, (g + 1) * POOL_GROUP)
        csg = cs[:, :, sl]
        lagged = jnp.pad(csg[:, :s - w + 1], ((0, 0), (w - 1, 0), (0, 0)))
        count = jnp.minimum(t1, float(w))
        mean = (csg[:, 1:] - lagged) / count[None, :, None]
        z = (mean - u32[:, :, sl]).astype(u.dtype)
        outs.append(jnp.einsum('bsc,cd->bsd', z, pool_w[g]))
    return jnp.concatenate(outs, axis=-1) * pool_scale

def second_inputs(seed: int = 0) -> dict:
    key = jax.random.key(seed)
    ks = jax.random.split(key, 10)
    x = jax.random.normal(ks[0], (BATCH, SEQ, D_MODEL), jnp.float32)
    w_in = jax.random.normal(ks[1], (DEPTH_2, D_MODEL, IN_W), jnp.float32) * D_MODEL ** -0.5
    b_f = jax.random.uniform(ks[2], (DEPTH_2, N_ATT_HEADS), jnp.float32, 1.0, 4.0)
    conv_w = jax.random.normal(ks[3], (DEPTH_2, CONV_TAPS, CONV_W), jnp.float32) * CONV_TAPS ** -0.5
    pool_w = jax.random.normal(ks[4], (DEPTH_2, len(POOL_WINDOWS), POOL_GROUP, POOL_GROUP),
                               jnp.float32) * POOL_GROUP ** -0.5
    pool_scale = 1.0 + 0.1 * jax.random.normal(ks[5], (DEPTH_2, POOL_W), jnp.float32)
    w_out = jax.random.normal(ks[6], (DEPTH_2, MIX_W, D_MODEL), jnp.float32) * (
        MIX_W ** -0.5 * DEEPNORM_BETA)
    ln_g = 1.0 + 0.1 * jax.random.normal(ks[7], (DEPTH_2, D_MODEL), jnp.float32)
    ln_b = 0.02 * jax.random.normal(ks[8], (DEPTH_2, D_MODEL), jnp.float32)
    return {"x": x, "w_in": w_in, "b_f": b_f, "conv_w": conv_w, "pool_w": pool_w,
            "pool_scale": pool_scale, "w_out": w_out, "ln_g": ln_g, "ln_b": ln_b}

def second_block(x, w_in, b_f, conv_w, pool_w, pool_scale, w_out, ln_g, ln_b):
    b, s, _ = x.shape
    for l in range(DEPTH_2):
        proj = jnp.einsum('bsd,de->bse', x, w_in[l])
        (q, k, v, g_att, fg, c_b, c_c, c_h, g_conv, p_u, g_pool) = jnp.split(
            proj, IN_SPLITS, axis=-1)
        heads = (b, s, N_ATT_HEADS, HEAD_DIM)
        y_att = forgetting_attention(q.reshape(heads), k.reshape(heads), v.reshape(heads),
                                     fg, b_f[l]) * jax.nn.silu(g_att)
        y_conv = short_conv_mixer(c_b, c_c, c_h, conv_w[l]) * jax.nn.silu(g_conv)
        y_pool = multiscale_pool_mixer(p_u, pool_w[l], pool_scale[l]) * jax.nn.silu(g_pool)
        y = jnp.concatenate([y_att, y_conv, y_pool], axis=-1)
        y = jnp.einsum('bse,ed->bsd', y, w_out[l])
        x = layer_norm_2(DEEPNORM_ALPHA * x + y, ln_g[l], ln_b[l])
    return x


def setup_inputs(seed=0):
    out = dict(first_inputs(seed))
    for name, value in second_inputs(seed + 1).items():
        if name != "x":
            out[name + "_2"] = value
    return out


def reference(
    x, even_norm, even_w_in, even_conv, even_a_log, even_dt_bias, even_sinks, even_onorm,
    even_w_out, odd_norm, odd_w_in, odd_ln_g, odd_ln_b, odd_w_s, odd_b_s, odd_w_out, ffn_norm,
    ffn_w_gate, ffn_w_up, ffn_w_down, final_norm, w_in_2, b_f_2, conv_w_2, pool_w_2,
    pool_scale_2, w_out_2, ln_g_2, ln_b_2,
):
    x = first_block(
        x, even_norm, even_w_in, even_conv, even_a_log, even_dt_bias, even_sinks, even_onorm,
        even_w_out, odd_norm, odd_w_in, odd_ln_g, odd_ln_b, odd_w_s, odd_b_s, odd_w_out,
        ffn_norm, ffn_w_gate, ffn_w_up, ffn_w_down, final_norm,
    )
    return second_block(
        x, w_in_2, b_f_2, conv_w_2, pool_w_2, pool_scale_2, w_out_2, ln_g_2, ln_b_2,
    )


_drawn_inputs = setup_inputs


def setup_inputs(seed=0):
    import zlib

    import numpy as np

    out = dict(_drawn_inputs(seed))
    spreads = {}
    factors = {'even_dt_bias': 5.907,
     'even_sinks': 2.96,
     'odd_ln_g': 3.348,
     'odd_ln_b': 8.0,
     'b_f_2': 30.072,
     'pool_scale_2': 4.581,
     'ln_b_2': 2.761}
    for name, (base, spread) in spreads.items():
        noise = np.random.default_rng([zlib.crc32(name.encode()), seed]).standard_normal(out[name].shape)
        drawn = base * np.exp(spread * noise) if base else spread * noise
        out[name] = __import__('jax').numpy.asarray(drawn.astype(out[name].dtype))
    for name, factor in factors.items():
        out[name] = (out[name] * factor).astype(out[name].dtype)
    return out
```

```python
from contextlib import ExitStack

import numpy as np

import concourse.bass as bass
from concourse import mybir

ACT = mybir.ActivationFunctionType
ALU = mybir.AluOpType
AX = mybir.AxisListType
F32 = mybir.dt.float32
F32R = mybir.dt.float32r

P = 128
D = 2048
SEQ = 256
NT = SEQ // P
KT = D // P
BLK = 512
DFF = 5632
FKT = DFF // P
NPAIR = DFF // BLK
EPS = 1e-6
LN2_EPS = 1e-5
ALPHA = 2.0 ** 0.25
A_Q, A_KV, A_HD = 1024, 128, 64
B_HEADS, B_HD = 8, 128
NEG = -1e30

C_IDENT, C_UPPER, C_ONES, C_PREV, C_CAUSAL, C_STRICT, C_LEVEL = [P * i for i in range(7)]
LEVELS = 7
N_CONST = C_LEVEL + LEVELS * P
POOL_WINDOWS = (2, 4, 8, 16)


def shape_constants():
    i = np.arange(P)[:, None]
    j = np.arange(P)[None, :]
    f = np.float32
    parts = [
        (i == j).astype(f), (i <= j).astype(f), np.ones((P, P), f),
        np.where(j > i, 0.0, NEG).astype(f),
        np.where(j <= i, 0.0, NEG).astype(f),
        (i > j).astype(f),
    ]
    for level in range(LEVELS):
        s = 1 << level
        parts.append(((i // (2 * s) == j // (2 * s)) & (i // s > j // s)).astype(f))
    consts = np.concatenate(parts, axis=1)
    s = np.arange(SEQ)[:, None]
    t = np.arange(SEQ)[None, :]
    pool = np.stack([((t - s >= 0) & (t - s < w)) / np.minimum(t + 1.0, float(w)) - (s == t)
                     for w in POOL_WINDOWS], axis=1).astype(f)
    return consts, pool


ROWS_A = (("even_norm", 16), ("ffn0_norm", 16), ("ffn1_norm", 16), ("odd_norm", 16),
          ("final_norm", 16), ("pool_scale", 4), ("conv2", 12), ("b_s", 8))
COL = {}
_at = 0
for _n, _r in ROWS_A:
    COL[_n] = _at
    _at += _r
N_ROWS_A = _at
COL["conv"] = _at
N_ROWS_B = 96
N_COLS = N_ROWS_A + N_ROWS_B
NORMS = ("even_norm", "ffn0_norm", "odd_norm", "ffn1_norm", "final_norm")


class Block:

    def __init__(self, kind, j, pieces, width, nk=KT, lhs="x"):
        self.kind, self.j, self.pieces, self.width, self.nk, self.lhs = kind, j, pieces, width, nk, lhs
        self.groups = [4] * (nk // 4) if nk == KT else [4, 4, 3] * (nk // 11)


ACT_KINDS = ("z", "gate", "v", "u", "ga", "gc", "gp")
SPLIT_KINDS = ("resid", "up", "u")
COPY_KINDS = ("conv", "k2", "q2", "ch", "gc", "gp")


T_INIT = KT // 2
PHASE = {"kvba": 0, "qa": 0, "conv": 0, "z": 0, "resid": 1, "gate": 2, "up": 2, "v": 3, "u": 3,
         "fg": 4, "k2": 4, "q2": 4, "v2": 4, "ga": 4, "cc": 4, "ch": 4, "cb": 4, "gc": 4, "pu": 4, "gp": 4,
         "final": 5}


def plan(w):
    out = []
    e = w["even_w_in"]
    kv = A_Q
    out.append(Block("kvba", 0, [(e, kv, 256, 0), (e, 5376, 16, 256)], 272))
    out += [Block("qa", j, [(e, BLK * j, BLK, 0)], BLK) for j in range(2)]
    out += [Block("conv", j, [(e, 1280 + BLK * j, BLK, 0)], BLK) for j in range(6)]
    out += [Block("z", j, [(e, 4352 + BLK * j, BLK, 0)], BLK) for j in range(2)]
    out += [Block("resid", j, [(w["even_w_out"], BLK * j, BLK, 0)], BLK, lhs="f") for j in range(4)]

    def ffn(n):
        for i in range(NPAIR):
            out.append(Block("gate", i, [(w[f"gate{n}"], BLK * i, BLK, 0)], BLK))
            out.append(Block("up", i, [(w[f"up{n}"], BLK * i, BLK, 0)], BLK))
        for j in range(4):
            out.append(Block("resid", j, [(w[f"down{n}"], BLK * j, BLK, 0)], BLK, nk=FKT, lhs="f"))

    ffn(0)
    o = w["odd_w_in"]
    out.extend(Block("v", j, [(o, D + BLK * j, BLK, 0)], BLK) for j in range(4))
    out.extend(Block("u", j, [(o, BLK * j, BLK, 0)], BLK) for j in range(4))
    out.extend(Block("resid", j, [(w["odd_w_out"], BLK * j, BLK, 0)], BLK, lhs="f") for j in range(4))
    ffn(1)
    s = w["w_in_2"]
    for kind, j, c, n in (("fg", 0, 4096, 8), ("k2", 0, 1024, BLK), ("q2", 0, 0, BLK), ("v2", 0, 2048, BLK),
                          ("ga", 0, 3072, BLK), ("k2", 1, 1536, BLK), ("q2", 1, BLK, BLK), ("v2", 1, 2560, BLK),
                          ("ga", 1, 3584, BLK), ("cc", 0, 4616, BLK), ("ch", 0, 5128, BLK), ("cb", 0, 4104, BLK),
                          ("gc", 0, 5640, BLK), ("pu", 0, 6152, BLK), ("gp", 0, 6664, BLK)):
        out.append(Block(kind, j, [(s, c, n, 0)], n))
    out.extend(Block("final", j, [(w["w_out_2"], BLK * j, BLK, 0)], BLK, lhs="f") for j in range(4))

    g = k = norm = n_act = n_dve = 0
    t, s = T_INIT, T_INIT
    ends = []
    for b, blk in enumerate(out):
        if blk.kind == "resid" and blk.j == 0 and norm == 0:
            t, s = t + T_INIT, s + T_INIT
            blk.mix_t0 = t - T_INIT
        blk.b, blk.g0, blk.k0, blk.t0, blk.h0, blk.norm = b, g, k, t, s, norm
        blk.prev = out[b - 1] if b else None
        blk.slot_uses, blk.fkt = g // 4, 4 * blk.j
        blk.first = not b or PHASE[out[b - 1].kind] != PHASE[blk.kind]
        g += len(blk.groups)
        for n in blk.groups:
            k += n
            ends.append(k)
        blk.by_act = blk.kind in ACT_KINDS
        n_act += NT * blk.by_act
        n_dve += NT * (not blk.by_act)
        blk.n_act, blk.n_dve = n_act, n_dve
        t += 2 * (blk.kind in SPLIT_KINDS + COPY_KINDS)
        s += 2 * (blk.kind in SPLIT_KINDS)
        norm += blk.kind == "resid" and blk.j == 3
    return out, ends


class Later:

    def __init__(self, blk, it):
        self.kind, self.j, self.b, self.width, self.nk, self.lhs = blk.kind, blk.j, blk.b, blk.width, blk.nk, blk.lhs
        self.norm, self.groups, self.first, self.by_act = blk.norm, blk.groups, False, blk.by_act
        self.g0, self.k0 = blk.g0 + 8 * it, blk.k0 + 32 * it
        self.slot_uses = blk.g0 // 4 + 2 * it
        self.n_act, self.n_dve = blk.n_act + 2 * it, blk.n_dve + 2 * it
        self.t0, self.h0 = blk.t0 + 2 * it, blk.h0 + 2 * it
        self.fkt = 4 * it + 4 * blk.j
        self.cols = BLK * it


def program(nc, a, out):
    weights = {n: a[n].rearrange("(k p) n -> p k n", p=P) for n in (
        "even_w_in", "even_w_out", "odd_w_in", "odd_w_out", "w_in_2", "w_out_2")}
    for n in range(2):
        for key in ("gate", "up", "down"):
            weights[f"{key}{n}"] = a[f"ffn_w_{key}"][n].rearrange("(k p) n -> p k n", p=P)
    blocks, group_ends = plan(weights)
    by = {}
    for blk in blocks:
        by.setdefault(blk.kind, []).append(blk)
    even_resid, ffn_resid = by["resid"][0:4], (by["resid"][4:8], by["resid"][12:16])
    odd_resid = by["resid"][8:12]
    pairs = [[(by["gate"][n * NPAIR + i], by["up"][n * NPAIR + i]) for i in range(NPAIR)] for n in range(2)]
    heads_in = {blk.b: n for n, blk in enumerate(blocks[by["k2"][1].b:by["k2"][1].b + 8])}

    ctx = ExitStack()
    with ctx:
        def sem(name):
            return ctx.enter_context(nc.semaphore(name))

        def sb(name, shape, dt=F32):
            return ctx.enter_context(nc.sbuf_tensor(name, shape, dt))

        h = sb("h", [P, NT, D])
        raw = sb("raw", [P, 4, 4, BLK])
        w_hi = sb("w_hi", [P, 4, BLK], F32R)
        w_lo = sb("w_lo", [P, 4, BLK], F32R)
        gs = sb("gs", [P, NT, BLK])
        hb = sb("hb", [P, NT, BLK])
        consts = sb("consts_sb", [P, C_LEVEL])
        cols = sb("cols", [P, N_COLS])
        small = sb("small", [P, 168])
        stat = sb("stat", [P, 400])
        extra = sb("extra", [P, 8, SEQ])

        ident = consts[:, C_IDENT:C_IDENT + P]
        upper = consts[:, C_UPPER:C_UPPER + P]
        upper_ones = consts[:, C_UPPER:C_UPPER + 2 * P]
        ones = consts[:, C_ONES:C_ONES + P]
        m_causal = consts[:, C_CAUSAL:C_CAUSAL + P]
        m_window = consts[:, C_PREV:C_PREV + 2 * P]
        strict = consts[:, C_STRICT:C_STRICT + P]
        dt_bias, a_log, sinks = small[:, 0:8], small[:, 8:16], small[:, 16:32]
        onorm, b_f = small[:, 32:160], small[:, 160:168]

        used = [0]

        def st(*shape):
            n = int(np.prod(shape))
            v = stat[:, used[0]:used[0] + n]
            used[0] += n
            assert used[0] <= 400
            if len(shape) == 2:
                return v.rearrange("p (x y) -> p x y", x=shape[0])
            if len(shape) == 3:
                return v.rearrange("p (x y z) -> p x y z", x=shape[0], y=shape[1])
            return v

        neg_half = st(32)
        ssq, ms, rstd = st(5, NT, 4), st(2), st(5, NT)
        v_sum, v_mu, v_nmu, v_var, v_rstd = st(NT, 4), st(2), st(2), st(2), st(2)
        e_nm, e_es, e_sm, e_rd = st(2, 4), st(2, 4), st(2, 4), st(4)
        n_sinks = st(16)
        l2_ss, l2_r = st(2, NT, 8), st(2, NT, 8)
        ba, xa, xn, beta, g_log, gam, e_gam, k_scale = [st(NT, 8) for _ in range(8)]
        a_exp = st(8)
        o_ss, o_r, l2_q_r = st(8), st(8), st(NT, 8)
        f_nm, f_sm, f_rd = st(2), st(2), st(2)

        def overlay(*parts):
            got = []
            with ExitStack() as shared:
                for name, shape, *dt in parts:
                    got.append(shared.enter_context(nc.sbuf_tensor(name, shape, dt[0] if dt else F32)))
            return got

        xh, xl, fh, fl = overlay(("xh", [P, KT, SEQ], F32R), ("xl", [P, KT, SEQ], F32R),
                                 ("fh", [P, FKT, SEQ], F32R), ("fl", [P, FKT, SEQ], F32R))
        kd2, kTd, qaT, e_s, e_pT, _, _, qkv, S1, _, att, zs, dqT = overlay(
            ("kd2", [P, NT, 2, P]), ("kTd", [P, 2, SEQ]), ("qaT", [P, 8, SEQ]), ("e_s", [P, 2, 4 * SEQ]),
            ("e_pT", [P, 2, 4, P]), ("pad_e0", [P, 2048]), ("pad_e1", [P, 4096]), ("qkv", [P, 3, NT, 1024]),
            ("S1", [P, 8, P]), ("pad_e2", [P, 4096]), ("att", [P, NT, 1280]), ("zs", [P, NT, 1024]),
            ("dqT", [P, 8, SEQ]))
        dL, dQK, dD, dE, dY, dC, dkb, masks = overlay(
            *[(n, [P, 8, P]) for n in ("dL", "dQK", "dD", "dE", "dY", "dC", "dkb")],
            ("level_masks", [P, LEVELS, P]))
        _, v_nat, ln_g_row, wsT, _, mixed, ln_b_row, ws_nat = overlay(
            ("pad_o0", [P, 12288]), ("v_nat", [P, NT, D]), ("ln_g_row", [P, D]), ("wsT", [P, 8, P]),
            ("pad_o1", [P, 4096]), ("mixed", [P, NT, D]), ("ln_b_row", [P, D]), ("ws_nat", [P, 8, P]))
        _, kT2, qT2, v2, ycT, _, sga, pun, ccn, spT, hd_s, hd_pT, ya = overlay(
            ("pad_s0", [P, 12288]), ("kT2", [P, 8, SEQ]), ("qT2", [P, 8, SEQ]), ("v2", [P, NT, 1024]),
            ("ycT", [P, 4, SEQ]), ("pad_s1", [P, 4096]), ("sga", [P, NT, 1024]), ("pun", [P, NT, BLK]),
            ("ccn", [P, NT, BLK]), ("spT", [P, 4, SEQ]), ("hd_s", [P, 384]), ("hd_pT", [P, 3, P]),
            ("ya", [P, NT, P]))
        poolm, poolw, zT, gf_row = overlay(("poolm", [P, NT, 4, SEQ]), ("poolw", [P, 4, P]),
                                           ("zT", [P, 4, SEQ]), ("gf_row", [P, D]))
        fin, _, junk = overlay(("fin", [P, NT, D]), ("pad_j", [P, 4096]), ("junk", [P, D]))
        _, ln2_g_row, ln2_b_row = overlay(("pad_f0", [P, 12288]), ("ln2_g_row", [P, D]), ("ln2_b_row", [P, D]))
        conv_buf = gs[:, :, :].rearrange("p t (c n) -> p (t c) n", c=2)
        silu_buf = extra[:, 0:4, :]
        dkT = extra
        v_new = gs[:, :, :].rearrange("p t (c n) -> p (t c) n", c=4)
        q_dec = hb[:, :, :].rearrange("p t (c n) -> p (t c) n", c=4)
        cum_row = extra
        qn, kn, vn = qkv[:, 0], qkv[:, 1], qkv[:, 2]

        ps = ctx.enter_context(nc.psum_tensor("ps", [P, 8, BLK], F32))

        pooled = hb[:, :, :].rearrange("p t (c n) -> p (t c) n", c=2)

        def acc(blk, t):
            return ps[:, 2 * (blk.b % 2) + t, 0:blk.width]

        def halves(bank):
            return ps[:, bank, :].rearrange("p (k c) -> p k c", k=2)

        def quarters(first, n=1):
            return ps[:, first:first + n, :].rearrange("p b (k c) -> p (b k) c", k=4)

        x_loaded, const_loaded, rows_loaded, small_loaded = [sem(n) for n in (
            "x_loaded", "const_loaded", "rows_loaded", "small_loaded")]
        raw_ready = [sem(f"raw_ready{i}") for i in range(4)]
        hi_ready, lo_ready, mm_done = sem("hi_ready"), sem("lo_ready"), sem("mm_done")
        evac_act, evac_dve = sem("evac_act"), sem("evac_dve")
        turned, turned_hi, pt_read = sem("turned"), sem("turned_hi"), sem("pt_read")
        sq_done, ms_ready, rstd_ready = sem("sq_done"), sem("ms_ready"), sem("rstd_ready")
        pool_init, cols_t, cols_ready, dve_link, act_link = [sem(n) for n in (
            "pool_init", "cols_t", "cols_ready", "dve_link", "act_link")]
        conv_done, conv_silu, back_t, back_copied = [sem(n) for n in (
            "conv_done", "conv_silu", "back_t", "back_copied")]
        masks_loaded, kd_ready, a_turned, a_copied = [sem(n) for n in (
            "masks_loaded", "kd_ready", "a_turned", "a_copied")]
        scored, a_nm, a_exp_done, p_turned, p_copied, pv_done, a_out = [sem(n) for n in (
            "scored", "a_nm", "a_exp_done", "p_turned", "p_copied", "pv_done", "a_out")]
        l2_sq, l2_ms, l2_rs, l2_q, l2_k, d_turned, d_copied = [sem(n) for n in (
            "l2_sq", "l2_ms", "l2_rs", "l2_q", "l2_k", "d_turned", "d_copied")]
        g_in, g_act, g_ready, ug_ready, gam_mm, gam_ready = [sem(n) for n in (
            "g_in", "g_act", "g_ready", "ug_ready", "gam_mm", "gam_ready")]
        dec_in, dec_exp, kq_mm, lqk_ready, kv_ready = [sem(n) for n in (
            "dec_in", "dec_exp", "kq_mm", "lqk_ready", "kv_ready")]
        c_ready, y_mm, y_copied, de_mm, de_ready = [sem(n) for n in (
            "c_ready", "y_mm", "y_copied", "de_mm", "de_ready")]
        w_mm, w_copied, u_mm, vnew_ready, s_mm, s_ready, o_mm = [sem(n) for n in (
            "w_mm", "w_copied", "u_mm", "vnew_ready", "s_mm", "s_ready", "o_mm")]
        q_scale = sem("q_scale")
        o_sq, o_ms, o_rs, o_done = [sem(n) for n in ("o_sq", "o_ms", "o_rs", "o_done")]
        ln_loaded, ws_turned, ws_ready, v_stat, v_sq, v_ms, v_rs, v_done = [sem(n) for n in (
            "ln_loaded", "ws_turned", "ws_ready", "v_stat", "v_sq", "v_ms", "v_rs", "v_done")]
        mix_mm, mix_out, gated = sem("mix_mm"), sem("mix_out"), sem("gated")
        f_in, f_act, f_lf, f_mm, f_copied = [sem(n) for n in ("f_in", "f_act", "f_lf", "f_mm", "f_copied")]
        h_scored, h_nm, h_exp, h_pt, h_ptc, h_pv, h_ya, h_yt, h_hi, h_lo = [sem(n) for n in (
            "h_scored", "h_nm", "h_exp", "h_pt", "h_ptc", "h_pv", "h_ya", "h_yt", "h_hi", "h_lo")]
        yc_conv, yc_ready, yc_hi, yc_lo = sem("yc_conv"), sem("yc_ready"), sem("yc_hi"), sem("yc_lo")
        pool_loaded, z_mm, z_copied, pw_mm, yp_ready, yp_hi, yp_lo = [sem(n) for n in (
            "pool_loaded", "z_mm", "z_copied", "pw_mm", "yp_ready", "yp_hi", "yp_lo")]
        gf_loaded, ln2_loaded, x_out, r_stat, r_sq, r_ms, r_rs, fin_ready, stored = [sem(n) for n in (
            "gf_loaded", "ln2_loaded", "x_out", "r_stat", "r_sq", "r_ms", "r_rs", "fin_ready", "stored")]

        def k_slots(blk):
            k = 0
            for gi, n in enumerate(blk.groups):
                for kk in range(n):
                    yield k, gi % 4, kk, gi
                    k += 1

        def run_blocks(eng, stream, mix):
            b = 0
            while b < len(blocks):
                blk = blocks[b]
                if blk.kind == "resid" and blk.lhs == "f" and blk is even_resid[0]:
                    mix()
                if blk.kind == "gate" and blk.j == 1:
                    n = 0 if blk is pairs[0][1][0] else 1
                    gate, up = pairs[n][1]
                    last_up = pairs[n][0][1]
                    with eng.Fori(0, NPAIR - 1) as it:
                        g, u, lu = Later(gate, it), Later(up, it), Later(last_up, it)
                        stream(g, lu)
                        stream(u, g)
                    b += 2 * (NPAIR - 1)
                    continue
                stream(blk, None if blk is even_resid[0] else blk.prev)
                b += 1

        def linker(eng, s):
            n = [0]

            def link(ins):
                n[0] += 1
                ins.then_inc(s, 1)
                eng.wait_ge(s, n[0])
            return link

        def lf_rows(t):
            return (gs if t == 0 else ccn)[:, :, :].rearrange("p t (c n) -> p (t c) n", c=4)

        def head_rows(t):
            return hd_s[:, 0:P] if t == 0 else hd_s[:, P:3 * P]

        def u_hooks(blk):
            return (8, 9, 10, 13) if blk.j == 0 else (3, 3, 4, 7)

        block = ctx.enter_context(nc.Block())

        @block.sync
        def _(sp):
            sp.dma_start(consts[:], a["consts"][:, 0:C_LEVEL]).then_inc(const_loaded, 16)
            x_rows = a["x"].rearrange("b (t p) d -> p (b t) d", p=P)
            for t in range(NT):
                sp.dma_start(h[:, t, :], x_rows[:, t, :]).then_inc(x_loaded, 16)

            def load(blk, _prev):
                k = 0
                for gi, n in enumerate(blk.groups):
                    if isinstance(blk, Later):
                        sp.wait_ge(lo_ready, blk.k0 + k - 12)
                    elif blk.g0 + gi >= 4:
                        sp.wait_ge(lo_ready, group_ends[blk.g0 + gi - 4])
                    for w, col, width, at in pieces_of(blk):
                        sp.dma_start(raw[:, gi % 4, 0:n, at:at + width],
                                     w[:, k:k + n, bass.ds(col, width)]).then_inc(raw_ready[gi % 4], 16)
                    k += n

            def pieces_of(blk):
                if isinstance(blk, Later):
                    w, col, width, at = blocks[blk.b].pieces[0]
                    return [(w, col + blk.cols, width, at)]
                return blk.pieces

            run_blocks(sp, load, lambda: None)

        @block.scalar
        def _(act):
            link = linker(act, act_link)
            for name, n in ROWS_A:
                src = {"even_norm": a["even_norm"], "ffn0_norm": a["ffn_norm"][0:1], "ffn1_norm": a["ffn_norm"][1:2],
                       "odd_norm": a["odd_norm"], "final_norm": a["final_norm"], "pool_scale": a["pool_scale_2"],
                       "conv2": a["conv_w_2"], "b_s": a["odd_b_s"]}[name]
                pattern = {"final_norm": "(k c) -> k c", "conv2": "a t (k c) -> (a t k) c",
                           "b_s": "a k c -> (a k) c"}.get(name, "a (k c) -> (a k) c")
                kw = {} if name == "b_s" else {"c": P}
                act.dma_start(hb[COL[name]:COL[name] + n, 0, 0:P], src.rearrange(pattern, **kw)).then_inc(rows_loaded, 16)
            act.dma_start(hb[0:N_ROWS_B, 1, 0:P],
                          a["even_conv"].rearrange("a t (k c) -> (a t k) c", c=P)).then_inc(rows_loaded, 16)
            for dst, src, n in ((dt_bias, a["even_dt_bias"], 8), (a_log, a["even_a_log"], 8),
                                (sinks, a["even_sinks"], 16), (onorm, a["even_onorm"], P), (b_f, a["b_f_2"], 8)):
                act.dma_start(dst, src.to_broadcast([P, n])).then_inc(small_loaded, 16)
            def square(norm, j, t):
                n = 8 * norm + 2 * j + t if norm else 4 * t + j
                if n:
                    act.wait_ge(sq_done, n)
                act.activation(gs[:, t, :], h[:, t, BLK * j:BLK * (j + 1)], ACT.Square,
                               accum_out=ssq[:, norm, t, j:j + 1]).then_inc(sq_done, 1)

            act.wait_ge(x_loaded, 16 * NT)
            for t in range(NT):
                for j in range(4):
                    square(0, j, t)

            def split_x(gain, kt, c, t0, h0):
                act.wait_ge(turned, t0 + c + 1)
                for kk in range(2):
                    ins = act.activation(xh[:, kt + kk, :], halves(4 + c)[:, kk, :], ACT.Copy,
                                         scale=cols[:, gain + kt + kk:gain + kt + kk + 1])
                ins.then_inc(turned_hi, 1)

            act.wait_ge(cols_ready, 1)
            for m in range(T_INIT):
                split_x(COL["even_norm"], 2 * m, m % 2, m - m % 2, 0)

            def finished(p):
                act.wait_ge(mm_done, p.k0 + p.nk)

            def after(p, k, blk):
                if p.kind == "z" and k == 3:
                    finished(p)
                    for t in range(NT):
                        act.activation(zs[:, t, BLK * p.j:BLK * (p.j + 1)], acc(p, t), ACT.Silu,
                                       scale=rstd[:, 0, t:t + 1]).then_inc(evac_act, 1)
                if p.kind == "conv" and k in (8, 10, 12, 14):
                    j = (k - 8) // 2
                    act.wait_ge(conv_done, 4 * p.j + j + 1)
                    if p.j:
                        act.wait_ge(back_t, 2 * p.j)
                    act.activation(silu_buf[:, j, :], conv_buf[:, j, :], ACT.Silu).then_inc(conv_silu, 1)
                pp = p.prev if not isinstance(p, Later) else None
                if pp is not None and pp.kind == "conv" and k == 2:
                    for t in range(NT):
                        act.wait_ge(back_t, 2 * pp.j + t + 1)
                        act.copy(qkv[:, pp.j // 2, t, BLK * (pp.j % 2):BLK * (pp.j % 2 + 1)],
                                 ps[:, 6 + t, :]).then_inc(back_copied, 1)
                if p.kind == "gate" and k == 3:
                    finished(p)
                    act.wait_ge(rstd_ready, p.norm + 1)
                    act.wait_ge(evac_dve, p.n_dve)
                    for t in range(NT):
                        act.activation(gs[:, t, :], acc(p, t), ACT.Silu,
                                       scale=rstd[:, p.norm, t:t + 1]).then_inc(evac_act, 1)
                if p.kind == "up" and k == 7:
                    for c in range(2):
                        act.wait_ge(turned, p.t0 + c + 1)
                        act.copy(fh[:, bass.ds(p.fkt + 2 * c, 2), :], halves(4 + c)).then_inc(turned_hi, 1)
                if p.kind == "resid":
                    if k == 4:
                        act.wait_ge(evac_dve, p.n_dve)
                        for t in range(NT):
                            square(p.norm + 1, p.j, t)
                    if k == 7:
                        for c in range(2):
                            split_x(COL[NORMS[p.norm + 1]], 4 * p.j + 2 * c, c, p.t0, p.h0)
                if p.kind == "v" and k == 3:
                    finished(p)
                    act.wait_ge(rstd_ready, p.norm + 1)
                    for t in range(NT):
                        act.activation(v_nat[:, t, BLK * p.j:BLK * (p.j + 1)], acc(p, t), ACT.Gelu,
                                       scale=rstd[:, p.norm, t:t + 1],
                                       accum_out=v_sum[:, t, p.j:p.j + 1]).then_inc(evac_act, 1)
                if p.kind == "v" and p.j == 3 and k in (5, 6):
                    t = k - 5
                    act.wait_ge(v_stat, 1)
                    act.activation(mixed[:, t, :], v_nat[:, t, :], ACT.Square, bias=v_nmu[:, t:t + 1],
                                   accum_out=v_var[:, t:t + 1]).then_inc(v_sq, 1)
                if p.kind == "u":
                    ka, _, _, kc = u_hooks(p)
                    if p.j == 0 and k in (5, 7, 9, 11):
                        pair = (k - 5) // 2
                        act.wait_ge(mix_mm, pair + 1)
                        for t in range(NT):
                            for gg in range(2):
                                g = 2 * pair + gg
                                act.activation(mixed[:, t, 256 * g:256 * (g + 1)], halves(6 + t)[:, gg, :],
                                               ACT.Identity, bias=cols[:, COL["b_s"] + g:COL["b_s"] + g + 1]
                                               ).then_inc(mix_out, 1)
                    if k == ka:
                        finished(p)
                        if p.j:
                            act.wait_ge(gated, 2 * p.j)
                        for t in range(NT):
                            act.activation(gs[:, t, :], acc(p, t), ACT.Gelu,
                                           scale=rstd[:, p.norm, t:t + 1]).then_inc(evac_act, 1)
                    if k == kc:
                        for c in range(2):
                            act.wait_ge(turned, p.t0 + c + 1)
                            act.copy(fh[:, 4 * p.j + 2 * c:4 * p.j + 2 * c + 2, :],
                                     halves(4 + c)).then_inc(turned_hi, 1)
                if p.kind in ("ga", "gc", "gp") and k == 3:
                    finished(p)
                    if p.kind == "gc":
                        act.wait_ge(f_mm, 5)
                    if p.kind == "gp":
                        act.wait_ge(gated, 10)
                    for t in range(NT):
                        dst = sga[:, t, BLK * p.j:BLK * (p.j + 1)] if p.kind == "ga" else gs[:, t, :]
                        act.activation(dst, acc(p, t), ACT.Silu,
                                       scale=rstd[:, 4, t:t + 1]).then_inc(evac_act, 1)
                if p.kind == "gc" and k == 8:
                    act.wait_ge(yc_ready, 2)
                    act.copy(fh[:, 8:12, :], ycT[:, :, :]).then_inc(yc_hi, 1)
                if p.kind == "fg" and k == 5:
                    act.wait_ge(f_in, 1)
                    link(act.activation(xn[:, :, :], xn[:, :, :], ACT.Exp))
                    act.activation(xn[:, :, :], xn[:, :, :], ACT.Ln, bias=1.0).then_inc(f_act, 1)
                if p.kind == "final" and k == 4:
                    act.wait_ge(evac_dve, p.n_dve)
                    for t in range(NT):
                        act.activation(gs[:, t, :], h[:, t, BLK * p.j:BLK * (p.j + 1)], ACT.Identity,
                                       accum_out=v_sum[:, t, p.j:p.j + 1]).then_inc(r_stat, 1)

            def during(blk, k):
                if blk.kind == "v" and blk.j == 0 and k == 3:
                    act.wait_ge(mm_done, blk.k0)
                    act.dma_start(ws_nat[:, :, :], a["odd_w_s"][0].rearrange("g t s -> t g s")).then_inc(ln_loaded, 16)
                    act.dma_start(ln_g_row[:, :], a["odd_ln_g"].to_broadcast([P, D])).then_inc(ln_loaded, 16)
                    act.dma_start(ln_b_row[:, :], a["odd_ln_b"].to_broadcast([P, D])).then_inc(ln_loaded, 16)
                if blk.b in heads_in:
                    n = heads_in[blk.b]
                    if k == 6:
                        act.wait_ge(h_nm, n + 1)
                        for t in range(NT):
                            act.activation(head_rows(t), head_rows(t), ACT.Exp, bias=f_nm[:, t:t + 1],
                                           accum_out=f_sm[:, t:t + 1]).then_inc(h_exp, 1)
                    if k == 9:
                        act.wait_ge(h_pt, n + 1)
                        act.copy(hd_pT[:, :, :], ps[:, 7, 0:3 * P].rearrange("p (c q) -> p c q", c=3)).then_inc(h_ptc, 1)
                    if k == 14:
                        act.wait_ge(h_yt, n + 1)
                        act.copy(fh[:, n, :], ps[:, 7, 0:SEQ]).then_inc(h_hi, 1)
                if blk.kind == "final" and blk.j == 0:
                    if k == 0:
                        act.wait_ge(mm_done, blk.k0)
                        act.dma_start(poolm[:, :, :, :], a["pool_consts"].rearrange("(t p) w q -> p t w q", p=P)
                                      ).then_inc(pool_loaded, 16)
                        act.dma_start(poolw[:, :, :], a["pool_w_2"][0].rearrange("g c d -> c g d")).then_inc(pool_loaded, 16)
                        act.dma_start(gf_row[:, :], a["final_norm"].unsqueeze(0).to_broadcast([P, D])).then_inc(gf_loaded, 16)
                        act.wait_ge(h_pv, 8)
                        act.dma_start(ln2_g_row[:, :], a["ln_g_2"].to_broadcast([P, D])).then_inc(ln2_loaded, 16)
                        act.dma_start(ln2_b_row[:, :], a["ln_b_2"].to_broadcast([P, D])).then_inc(ln2_loaded, 16)
                    if k == 11:
                        act.wait_ge(yp_ready, 4)
                        act.copy(fh[:, 12:16, :], pooled).then_inc(yp_hi, 1)

            def stream(blk, p):
                for k, slot, kk, gi in k_slots(blk):
                    if kk == 0:
                        act.wait_ge(raw_ready[slot], 16 * (blk.slot_uses + gi // 4 + 2))
                    if blk.b or k > 3:
                        act.wait_ge(mm_done, blk.k0 + k - 3)
                    act.copy(w_hi[:, k % 4, 0:blk.width], raw[:, slot, kk, 0:blk.width]).then_inc(hi_ready, 1)
                    if p is not None:
                        after(p, k, blk)
                    during(blk, k)

            def mix():
                z1 = by["z"][1]
                after(z1, 3, None)
                act.wait_ge(mm_done, z1.k0 + z1.nk)
                act.dma_start(masks[:, :, :], a["consts"][:, C_LEVEL:N_CONST].rearrange("p (l c) -> p l c", l=LEVELS)
                              ).then_inc(masks_loaded, 16)
                act.wait_ge(a_turned, 1)
                act.copy(kTd[:, :, :], halves(4)).then_inc(a_copied, 1)
                for m, bank in enumerate((5, 0, 1, 2)):
                    act.wait_ge(a_turned, m + 2)
                    act.copy(qaT[:, 2 * m:2 * m + 2, :], halves(bank)).then_inc(a_copied, 1)
                for u in range(9):
                    if u < 8:
                        w = P if u < 4 else 2 * P
                        act.wait_ge(a_nm, u + 1)
                        for i in range(4):
                            act.activation(e_s[:, u % 2, w * i:w * (i + 1)], e_s[:, u % 2, w * i:w * (i + 1)],
                                           ACT.Exp, bias=e_nm[:, u % 2, i:i + 1],
                                           accum_out=e_sm[:, u % 2, i:i + 1])
                        act.activation(e_es[:, u % 2, :], e_es[:, u % 2, :], ACT.Exp).then_inc(a_exp_done, 1)
                    if u >= 1:
                        act.wait_ge(p_turned, u)
                        for kb in range(1 if u <= 4 else 2):
                            ins = act.copy(e_pT[:, kb], quarters(4 + kb))
                        ins.then_inc(p_copied, 1)
                act.wait_ge(g_in, 1)
                link(act.activation(xn[:, :, :], xn[:, :, :], ACT.Exp))
                act.activation(xn[:, :, :], xn[:, :, :], ACT.Ln, bias=1.0)
                act.activation(a_exp, a_log, ACT.Exp)
                act.activation(beta[:, :, :], beta[:, :, :], ACT.Exp, scale=-1.0).then_inc(g_act, 1)
                for n, (src, t) in enumerate((s, t) for s in (qn, kn) for t in range(NT)):
                    if n >= 2:
                        act.wait_ge(l2_ms, n - 1)
                    act.activation((dD, dE)[n % 2][:, :, :], src[:, t, :].rearrange("p (h c) -> p h c", h=8),
                                   ACT.Square).then_inc(l2_sq, 1)
                for m in range(8):
                    act.wait_ge(d_turned, m + 1)
                    dst = (dqT if m < 4 else dkT)[:, 2 * (m % 4):2 * (m % 4) + 2, :]
                    act.copy(dst, halves(m % 4)).then_inc(d_copied, 1)
                for t in range(NT):
                    act.wait_ge(gam_ready, t + 1)
                    act.activation(e_gam[:, t, :], gam[:, t, :], ACT.Exp)
                    if t == 0:
                        act.activation(k_scale[:, 0, :], k_scale[:, 0, :], ACT.Exp)
                    else:
                        act.activation(q_dec[:, :, :], quarters(0, 2), ACT.Exp).then_inc(q_scale, 1)
                    act.wait_ge(dec_in, t + 1)
                    act.activation(dL[:, :, :], dY[:, :, :], ACT.Exp, scale=-1.0)
                    act.activation(dQK[:, :, :], dC[:, :, :], ACT.Exp).then_inc(dec_exp, 1)
                    for lv in range(1, LEVELS):
                        for half in range(2):
                            n = (t * (LEVELS - 1) + lv - 1) * 2 + half
                            act.wait_ge(y_mm, n + 1)
                            act.copy(dY[:, 4 * half:4 * half + 4, :], quarters(half)).then_inc(y_copied, 1)
                    if t == 1:
                        act.wait_ge(w_mm, 1)
                        act.mul(dY[:, :, :], quarters(2, 2), -1.0).then_inc(w_copied, 1)
                    else:
                        act.wait_ge(s_mm, 1)
                        act.copy(S1[:, :, :], quarters(2, 2)).then_inc(s_ready, 1)
                    act.wait_ge(o_mm, t + 1)
                    act.activation(dD[:, :, :], quarters(4, 2), ACT.Square).then_inc(o_sq, 1)
                for m in range(T_INIT):
                    act.wait_ge(turned, even_resid[0].mix_t0 + m + 1)
                    act.copy(fh[:, 2 * m:2 * m + 2, :], halves(4 + m % 2)).then_inc(turned_hi, 1)

            run_blocks(act, stream, mix)
            after(blocks[-1], 4, None)
            act.wait_ge(r_stat, 8 + 1)
            for t in range(NT):
                if t:
                    act.wait_ge(r_sq, t)
                act.activation(junk[:, :], h[:, t, :], ACT.Square, bias=v_nmu[:, t:t + 1],
                               accum_out=v_var[:, t:t + 1]).then_inc(r_sq, 1)
            out_rows = out.rearrange("b (t p) d -> p (b t) d", p=P)
            for n in range(4):
                t, c = n // 2, n % 2
                act.wait_ge(fin_ready, n + 1)
                act.dma_start(out_rows[:, t, 1024 * c:1024 * (c + 1)], fin[:, t, 1024 * c:1024 * (c + 1)]).then_inc(stored, 16)
            act.wait_ge(stored, 64)

        @block.tensor
        def _(pe):
            def turn(rows, t0):
                for c in range(2):
                    if not isinstance(t0, int) or t0 + c >= 2:
                        pe.wait_ge(pt_read, t0 + c - 1)
                    for kk in range(2):
                        for t in range(NT):
                            ins = pe.transpose(halves(4 + c)[:, kk, P * t:P * (t + 1)], rows(t, 2 * c + kk), ident)
                    ins.then_inc(turned, 1)

            def rows_of(buf, at=0):
                return lambda t, j: buf[:, t, at + P * j:at + P * (j + 1)]

            pe.wait_ge(const_loaded, 16)
            pe.wait_ge(rows_loaded, 16 * (len(ROWS_A) + 1))
            pe.transpose(ps[:, 6, 0:N_ROWS_A], hb[0:N_ROWS_A, 0, 0:P], ident[0:N_ROWS_A, 0:N_ROWS_A])
            pe.transpose(ps[:, 6, N_ROWS_A:N_COLS], hb[0:N_ROWS_B, 1, 0:P],
                         ident[0:N_ROWS_B, 0:N_ROWS_B]).then_inc(cols_t, 1)
            pe.wait_ge(x_loaded, 16 * NT)
            for j in range(4):
                turn(rows_of(h, BLK * j), 2 * j)

            def wait_stationary(blk, k):
                if blk.kind == "final":
                    if k < 8:
                        pe.wait_ge(h_lo, k + 1)
                    elif k in (8, 12):
                        pe.wait_ge(yc_lo if k == 8 else yp_lo, 1)
                    return
                t0 = {"kvba": lambda: 0, "gate": lambda: blk.prev.t0 - 6, "v": lambda: blk.prev.t0 - 6,
                      "fg": lambda: blk.prev.t0 - 6,
                      "resid": lambda: (blk.mix_t0 if blk is even_resid[0] else
                                        by["u"][0].t0 if blk is odd_resid[0] else
                                        pairs[0 if blk is ffn_resid[0][0] else 1][0][1].t0)}[blk.kind]()
                if k % 2 == 0:
                    pe.wait_ge(pt_read, t0 + k // 2 + 1)

            def after(p, k, blk):
                if p.kind == "conv" and k == 3:
                    pe.wait_ge(evac_dve, p.n_dve)
                    turn(rows_of(hb), p.t0)
                if p.kind == "conv" and k == 14:
                    pe.wait_ge(conv_silu, 4 * (p.j + 1))
                    if p.j:
                        pe.wait_ge(back_copied, 2 * p.j)
                    for t in range(NT):
                        for c in range(4):
                            ins = pe.transpose(ps[:, 6 + t, P * c:P * (c + 1)], silu_buf[:, c, P * t:P * (t + 1)], ident)
                        ins.then_inc(back_t, 1)
                if p.kind == "resid" and k == 3:
                    pe.wait_ge(evac_dve, p.n_dve)
                    turn(rows_of(h, BLK * p.j), p.t0)
                if p.kind in ("up", "ch", "k2", "q2") and k == 3:
                    pe.wait_ge(evac_dve, p.n_dve)
                    turn(rows_of(hb), p.t0)
                if p.kind == "u":
                    if p.j == 0 and k in (1, 3, 5, 7):
                        pair = (k - 1) // 2
                        if pair == 0:
                            pe.wait_ge(ws_ready, 1)
                            pe.wait_ge(v_done, 4)
                        else:
                            pe.wait_ge(mix_out, 4 * pair)
                        for t in range(NT):
                            for gg in range(2):
                                g = 2 * pair + gg
                                ins = pe.matmul(halves(6 + t)[:, gg, :], wsT[:, g, :],
                                                v_nat[:, t, 256 * g:256 * (g + 1)], start=True, stop=True)
                        ins.then_inc(mix_mm, 1)
                    if k == u_hooks(p)[2]:
                        pe.wait_ge(gated, 2 * (p.j + 1))
                        turn(rows_of(hb), p.t0)
                if p.kind == "gc" and k == 4:
                    pe.wait_ge(gated, 10)
                    turn(rows_of(hb), p.t0)
                if p.kind == "gp" and k == 4:
                    pe.wait_ge(evac_act, p.n_act)
                    turn(rows_of(gs), p.t0)
                if p.kind == "fg" and k == 8:
                    pe.wait_ge(f_lf, 1)
                    pe.matmul(ps[:, 7, 0:8], upper, xa[:, 0, :], start=True, stop=True)
                    pe.matmul(ps[:, 7, 8:16], ones, xa[:, 0, :], start=True, stop=False)
                    pe.matmul(ps[:, 7, 8:16], upper, xa[:, 1, :], start=False, stop=True).then_inc(f_mm, 1)
                if p.kind == "k2" and p.j == 0 and k in (1, 4, 7, 10):
                    m = (k - 1) // 3
                    pe.wait_ge(f_lf, 3)
                    pe.wait_ge(f_copied, m)
                    for i in range(2):
                        dst = halves(6 + m % 2)[:, i, :]
                        pe.matmul(dst, lf_rows(0)[:, 2 * m + i, :], upper_ones, start=True, stop=False)
                        ins = pe.matmul(dst[:, P:2 * P], lf_rows(1)[:, 2 * m + i, :], upper, start=False, stop=True)
                    ins.then_inc(f_mm, 1)

            def during(blk, k):
                if blk.kind == "v" and blk.j == 1 and k == 3:
                    pe.wait_ge(ln_loaded, 48)
                    for g in range(8):
                        ins = pe.transpose(quarters(6, 2)[:, g, :], ws_nat[:, g, :], ident)
                    ins.then_inc(ws_turned, 1)
                if blk.b in heads_in:
                    n = heads_in[blk.b]
                    if k == 1:
                        pe.wait_ge(pt_read, by["q2"][n // 4].t0 + 2)
                        pe.wait_ge(f_copied, 5)
                        if n:
                            pe.wait_ge(h_ya, 2 * n)
                        pe.matmul(ps[:, 6, 0:P], qT2[:, n, 0:P], kT2[:, n, 0:P], start=True, stop=True)
                        pe.matmul(ps[:, 6, P:3 * P], qT2[:, n, P:2 * P], kT2[:, n, :],
                                  start=True, stop=True).then_inc(h_scored, 1)
                    if k == 5:
                        pe.wait_ge(h_exp, 2 * (n + 1))
                        if n:
                            pe.wait_ge(h_lo, n)
                        for c in range(3):
                            ins = pe.transpose(ps[:, 7, P * c:P * (c + 1)], hd_s[:, P * c:P * (c + 1)], ident)
                        ins.then_inc(h_pt, 1)
                    if k == 8:
                        pe.wait_ge(h_ptc, n + 1)
                        pe.wait_ge(evac_dve, by["v2"][n // 4].n_dve)
                        vh = slice(P * n, P * (n + 1))
                        pe.matmul(ps[:, 6, 0:P], hd_pT[:, 0, :], v2[:, 0, vh], start=True, stop=True)
                        pe.matmul(ps[:, 6, P:2 * P], hd_pT[:, 1, :], v2[:, 0, vh], start=True, stop=False)
                        pe.matmul(ps[:, 6, P:2 * P], hd_pT[:, 2, :], v2[:, 1, vh],
                                  start=False, stop=True).then_inc(h_pv, 1)
                    if k == 11:
                        pe.wait_ge(h_ya, 2 * (n + 1))
                        for t in range(NT):
                            ins = pe.transpose(ps[:, 7, P * t:P * (t + 1)], ya[:, t, :], ident)
                        ins.then_inc(h_yt, 1)
                if blk.kind == "final" and blk.j == 0:
                    if k == 2:
                        pe.wait_ge(pool_loaded, 32)
                        pe.wait_ge(evac_dve, by["pu"][0].n_dve)
                        for g in range(4):
                            for t in range(NT):
                                ins = pe.matmul(halves(6 + g // 2)[:, g % 2, :], pun[:, t, P * g:P * (g + 1)],
                                                poolm[:, t, g, :], start=(t == 0), stop=(t == 1))
                        ins.then_inc(z_mm, 1)
                    if k == 5:
                        pe.wait_ge(z_copied, 2)
                        for g in range(4):
                            ins = pe.matmul(halves(6 + g // 2)[:, g % 2, :], poolw[:, g, :], zT[:, g, :],
                                            start=True, stop=True)
                        ins.then_inc(pw_mm, 1)

            def stream(blk, p):
                if isinstance(blk, Later):
                    pe.wait_ge(*((evac_act, blk.n_act - 2) if blk.by_act else (evac_dve, blk.n_dve - 2)))
                elif blk.b >= 2:
                    old = blocks[blk.b - 2]
                    pe.wait_ge(*((evac_act, old.n_act) if old.by_act else (evac_dve, old.n_dve)))
                hi_x, lo_x = (xh, xl) if blk.lhs == "x" else (fh, fl)
                for k, _, _, _ in k_slots(blk):
                    if blk.first:
                        wait_stationary(blk, k)
                    pe.wait_ge(lo_ready, blk.k0 + k + 1)
                    hi_w, lo_w = w_hi[:, k % 4, 0:blk.width], w_lo[:, k % 4, 0:blk.width]
                    for t in range(NT):
                        tok = slice(P * t, P * (t + 1))
                        pe.matmul(acc(blk, t), hi_x[:, k, tok], hi_w, start=(k == 0), stop=False)
                        pe.matmul(acc(blk, t), hi_x[:, k, tok], lo_w, start=False, stop=False)
                        ins = pe.matmul(acc(blk, t), lo_x[:, k, tok], hi_w, start=False, stop=(k == blk.nk - 1))
                    ins.then_inc(mm_done, 1)
                    if p is not None:
                        after(p, k, blk)
                    during(blk, k)

            def mix():
                pe.wait_ge(kd_ready, 2)
                pe.wait_ge(evac_act, by["z"][1].n_act)
                pe.wait_ge(back_copied, 12)
                for g in range(2):
                    for t in range(NT):
                        ins = pe.transpose(halves(4)[:, g, P * t:P * (t + 1)], kd2[:, t, g, :], ident)
                ins.then_inc(a_turned, 1)
                for m, bank in enumerate((5, 0, 1, 2)):
                    for i in range(2):
                        for t in range(NT):
                            j = 2 * m + i
                            ins = pe.transpose(halves(bank)[:, i, P * t:P * (t + 1)], att[:, t, P * j:P * (j + 1)], ident)
                    ins.then_inc(a_turned, 1)
                pe.wait_ge(a_copied, 5)
                for u in range(9):
                    if u < 8:
                        grp, t = u % 4, u // 4
                        w = P * (t + 1)
                        if u >= 2:
                            pe.wait_ge(a_nm, u - 1)
                        for i in range(4):
                            hd = 4 * grp + 2 * (i % 2) + i // 2
                            rows = slice(64 * (hd % 2), 64 * (hd % 2) + 64)
                            ins = pe.matmul(ps[:, 2 * (u % 2) + i // 2, w * (i % 2):w * (i % 2 + 1)],
                                            qaT[rows, hd // 2, P * t:P * (t + 1)], kTd[rows, hd // 8, 0:w],
                                            start=True, stop=True)
                        ins.then_inc(scored, 1)
                    if u >= 1:
                        v = u - 1
                        grp, t = v % 4, v // 4
                        pe.wait_ge(a_exp_done, v + 1)
                        for kb in range(t + 1):
                            for i in range(4):
                                at = P * (t + 1) * i + P * kb
                                ins = pe.transpose(quarters(4 + kb)[:, i, :], e_s[:, v % 2, at:at + P], ident)
                        ins.then_inc(p_turned, 1)
                        pe.wait_ge(p_copied, v + 1)
                        if v >= 2:
                            pe.wait_ge(a_out, v - 1)
                        for i in range(4):
                            g = (4 * grp) // 8
                            for kb in range(t + 1):
                                ins = pe.matmul(ps[:, 6 + v % 2, 64 * i:64 * i + 64], e_pT[:, kb, i, :],
                                                att[:, kb, 1152 + 64 * g:1216 + 64 * g], start=(kb == 0), stop=(kb == t))
                        ins.then_inc(pv_done, 1)
                pe.wait_ge(a_out, 8)
                for m in range(8):
                    src = qn if m < 4 else kn
                    pe.wait_ge(l2_q if m < 4 else l2_k, 2)
                    if m >= 4:
                        pe.wait_ge(d_copied, m - 3)
                    for i in range(2):
                        for t in range(NT):
                            hd = 2 * (m % 4) + i
                            ins = pe.transpose(halves(m % 4)[:, i, P * t:P * (t + 1)], src[:, t, P * hd:P * (hd + 1)], ident)
                    ins.then_inc(d_turned, 1)
                pe.wait_ge(d_copied, 8)
                for t in range(NT):
                    tok = slice(P * t, P * (t + 1))
                    pe.wait_ge(ug_ready, t + 1)
                    if t:
                        pe.wait_ge(o_done, 1)
                    for half in range(2):
                        pe.matmul(ps[:, half, :], ones, dC[:, 4 * half:4 * half + 4, :], start=True, stop=True)
                    pe.matmul(ps[:, 4, 0:8], upper, g_log[:, t, :], start=True, stop=True).then_inc(gam_mm, 1)
                    for hd in range(8):
                        pe.matmul(quarters(2, 2)[:, hd, :], dkT[:, hd, tok], dkT[:, hd, tok], start=True, stop=True)
                        ins = pe.matmul(quarters(6, 2)[:, hd, :], dkT[:, hd, tok], dqT[:, hd, tok], start=True, stop=True)
                    ins.then_inc(kq_mm, 1)
                    for half in range(2):
                        pe.wait_ge(c_ready, LEVELS * t + 1)
                        pe.wait_ge(lqk_ready, t + 1)
                        for i in range(4):
                            ins = pe.matmul(quarters(4 + half)[:, i, :], dC[:, 4 * half + i, :], ident, start=True, stop=True)
                        ins.then_inc(de_mm, 1)
                    for lv in range(1, LEVELS):
                        for half in range(2):
                            pe.wait_ge(c_ready, LEVELS * t + lv + 1)
                            pe.wait_ge(de_ready, 2 * (LEVELS * t + lv - 1) + half + 1)
                            for i in range(4):
                                hd = 4 * half + i
                                ins = pe.matmul(quarters(half)[:, i, :], dC[:, hd, :], dE[:, hd, :], start=True, stop=True)
                            ins.then_inc(y_mm, 1)
                        for half in range(2):
                            pe.wait_ge(y_copied, 2 * ((LEVELS - 1) * t + lv - 1) + half + 1)
                            for i in range(4):
                                hd = 4 * half + i
                                if lv < LEVELS - 1:
                                    pe.matmul(quarters(2 + half)[:, i, :], dY[:, hd, :], dD[:, hd, :], start=True, stop=True)
                                ins = pe.matmul(quarters(4 + half)[:, i, :], dD[:, hd, :], dY[:, hd, :], start=True, stop=True)
                            ins.then_inc(de_mm, 1)
                    pe.wait_ge(de_ready, 2 * LEVELS * (t + 1))
                    pe.wait_ge(kv_ready, t + 1)
                    if t == 1:
                        for hd in range(8):
                            ins = pe.matmul(quarters(2, 2)[:, hd, :], dkb[:, hd, :], dE[:, hd, :], start=True, stop=True)
                        ins.then_inc(w_mm, 1)
                        pe.wait_ge(w_copied, 1)
                        pe.wait_ge(s_ready, 1)
                    for hd in range(8):
                        ins = pe.matmul(quarters(0, 2)[:, hd, :], dE[:, hd, :], vn[:, t, P * hd:P * (hd + 1)],
                                        start=True, stop=(t == 0))
                        if t == 1:
                            ins = pe.matmul(quarters(0, 2)[:, hd, :], dY[:, hd, :], S1[:, hd, :], start=False, stop=True)
                    ins.then_inc(u_mm, 1)
                    pe.wait_ge(vnew_ready, t + 1)
                    if t == 0:
                        for hd in range(8):
                            ins = pe.matmul(quarters(2, 2)[:, hd, :], dkb[:, hd, :], v_new[:, hd, :], start=True, stop=True)
                        ins.then_inc(s_mm, 1)
                    for hd in range(8):
                        if t == 1:
                            pe.matmul(quarters(4, 2)[:, hd, :], q_dec[:, hd, :], S1[:, hd, :], start=True, stop=False)
                        ins = pe.matmul(quarters(4, 2)[:, hd, :], dQK[:, hd, :], v_new[:, hd, :], start=(t == 0), stop=True)
                    ins.then_inc(o_mm, 1)
                pe.wait_ge(o_done, 2)
                for j in range(4):
                    turn(rows_of(att, BLK * j) if j < 2 else rows_of(qn, BLK * (j - 2)),
                         even_resid[0].mix_t0 + 2 * j)

            run_blocks(pe, stream, mix)

        @block.vector
        def _(dve):
            link = linker(dve, dve_link)
            STT, TT, TS = dve.scalar_tensor_tensor, dve.tensor_tensor, dve.tensor_scalar

            def spread(v, n, last=P):
                return v.unsqueeze(2).to_broadcast([P, n, last])

            def each(v, n):
                return v.unsqueeze(1).to_broadcast([P, n, v.shape[1]])

            def heads(v):
                return v.rearrange("p (h c) -> p h c", h=8)

            dve.wait_ge(cols_t, 1)
            dve.tensor_copy(cols[:, :], ps[:, 6, 0:N_COLS]).then_inc(cols_ready, 1)
            dve.wait_ge(cols_ready, 1)

            def low_x(gain, kt, c, h0):
                dve.wait_ge(turned_hi, h0 + c + 1)
                for kk in range(2):
                    ins = STT(xl[:, kt + kk, :], halves(4 + c)[:, kk, :], cols[:, gain + kt + kk:gain + kt + kk + 1],
                              xh[:, kt + kk, :].bitcast(F32), ALU.mult, ALU.subtract)
                ins.then_inc(pt_read, 1)

            for m in range(T_INIT):
                low_x(COL["even_norm"], 2 * m, m % 2, m - m % 2)

            def mean_square(n):
                dve.wait_ge(sq_done, 8 * (n + 1))
                if n:
                    dve.wait_ge(rstd_ready, n)
                link(dve.tensor_reduce(ms, ssq[:, n], AX.X, ALU.add))
                TS(ms, ms, 1.0 / D, EPS, ALU.mult, ALU.add).then_inc(ms_ready, 1)

            mean_square(0)

            def finished(p):
                dve.wait_ge(mm_done, p.k0 + p.nk)
                dve.wait_ge(rstd_ready, p.norm + 1)

            counts = {}

            def conv(j, taps, col, stride, src, dst, done, last_of_bank):
                for i in reversed(range(taps)):
                    lag = taps - 1 - i
                    w = cols[:, col + stride * i + j:col + stride * i + j + 1]
                    if lag == 0:
                        ins = TS(dst, src, w, None, ALU.mult)
                    else:
                        ins = STT(dst[:, lag:SEQ], src[:, 0:SEQ - lag], w, dst[:, lag:SEQ], ALU.mult, ALU.add)
                    if i:
                        link(ins)
                ins.then_inc(done, 1)
                if last_of_bank:
                    counts[done.name] = counts.get(done.name, 0) + 2
                    dve.wait_ge(done, counts[done.name])
                    dve.sem_inc(pt_read, 1)

            def after(p, k, blk):
                if p.kind == "kvba" and k == 3:
                    finished(p)
                    for t in range(NT):
                        r = rstd[:, 0, t:t + 1]
                        TS(att[:, t, A_Q:A_Q + 256], acc(p, t)[:, 0:256], r, None, ALU.mult)
                        TS(beta[:, t, :], acc(p, t)[:, 256:264], r, None, ALU.mult)
                        TS(xa[:, t, :], acc(p, t)[:, 264:272], r, None, ALU.mult).then_inc(evac_dve, 1)
                if p.kind == "qa" and k == 3:
                    finished(p)
                    for t in range(NT):
                        TS(att[:, t, BLK * p.j:BLK * (p.j + 1)], acc(p, t), rstd[:, 0, t:t + 1], None,
                           ALU.mult).then_inc(evac_dve, 1)
                if p.kind in ("conv", "k2", "q2") and k == 3:
                    finished(p)
                    dve.wait_ge(turned, p.t0)
                    for t in range(NT):
                        TS(hb[:, t, :], acc(p, t), rstd[:, p.norm, t:t + 1], None, ALU.mult).then_inc(evac_dve, 1)
                if p.kind == "conv" and k in (7, 9, 11, 13):
                    j = (k - 7) // 2
                    dve.wait_ge(turned, p.t0 + j // 2 + 1)
                    if p.j:
                        dve.wait_ge(conv_silu, 4 * (p.j - 1) + j + 1)
                    conv(4 * p.j + j, 4, COL["conv"], 24, halves(4 + j // 2)[:, j % 2, :], conv_buf[:, j, :],
                         conv_done, j % 2 == 1)
                if p.kind == "resid":
                    if k == 3:
                        dve.wait_ge(mm_done, p.k0 + p.nk)
                        for t in range(NT):
                            hs = h[:, t, BLK * p.j:BLK * (p.j + 1)]
                            TT(hs, acc(p, t), hs, ALU.add).then_inc(evac_dve, 1)
                    if k == 7:
                        for c in range(2):
                            low_x(COL[NORMS[p.norm + 1]], 4 * p.j + 2 * c, c, p.h0)
                    if k == 9 and p.j == 3:
                        mean_square(p.norm + 1)
                if p.kind == "up" and k == 3:
                    finished(p)
                    dve.wait_ge(evac_act, p.n_act)
                    dve.wait_ge(turned, p.t0)
                    for t in range(NT):
                        STT(hb[:, t, :], acc(p, t), rstd[:, p.norm, t:t + 1], gs[:, t, :], ALU.mult,
                            ALU.mult).then_inc(evac_dve, 1)
                if p.kind == "up" and k == 7:
                    low_f(p)
                if p.kind == "v" and p.j == 3 and k == 4:
                    dve.wait_ge(evac_act, p.n_act)
                    link(dve.tensor_reduce(v_mu, v_sum[:, :, :], AX.X, ALU.add))
                    link(TS(v_mu, v_mu, 1.0 / D, None, ALU.mult))
                    TS(v_nmu, v_mu, -1.0, None, ALU.mult).then_inc(v_stat, 1)
                if p.kind == "v" and p.j == 3 and k in (7, 8, 9, 10, 11, 12, 13, 14):
                    n = (k - 7) % 4
                    t, part = n // 2, slice(1024 * (n % 2), 1024 * (n % 2 + 1))
                    if k < 11:
                        dve.wait_ge(v_sq, t + 1)
                        dve.wait_ge(ln_loaded, 48)
                        STT(v_nat[:, t, part], v_nat[:, t, part], v_mu[:, t:t + 1], ln_g_row[:, part], ALU.subtract,
                            ALU.mult).then_inc(v_done, 1)
                    else:
                        dve.wait_ge(v_rs, 1)
                        dve.wait_ge(v_done, 4)
                        STT(v_nat[:, t, part], v_nat[:, t, part], v_rstd[:, t:t + 1], ln_b_row[:, part], ALU.mult,
                            ALU.add).then_inc(v_done, 1)
                    if k == 8:
                        dve.wait_ge(v_sq, 2)
                        TS(v_var, v_var, 1.0 / D, EPS, ALU.mult, ALU.add).then_inc(v_ms, 1)
                if p.kind == "u":
                    _, kb, _, kc = u_hooks(p)
                    if k == kb:
                        dve.wait_ge(evac_act, p.n_act)
                        dve.wait_ge(mix_out, 16 if p.j else 4)
                        dve.wait_ge(turned, p.t0)
                        for t in range(NT):
                            TT(hb[:, t, :], gs[:, t, :], mixed[:, t, BLK * p.j:BLK * (p.j + 1)],
                               ALU.mult).then_inc(gated, 1)
                    if k == kc:
                        low_f(p)
                if p.kind == "fg":
                    if k == 3:
                        finished(p)
                        for t in range(NT):
                            TS(xa[:, t, :], acc(p, t), rstd[:, 4, t:t + 1], None, ALU.mult).then_inc(evac_dve, 1)
                    if k == 4:
                        dve.wait_ge(evac_dve, p.n_dve)
                        link(TT(xa[:, :, :], xa[:, :, :], each(b_f, NT), ALU.add))
                        minus_abs().then_inc(f_in, 1)
                    if k == 6:
                        dve.wait_ge(f_act, 1)
                        STT(xa[:, :, :], xa[:, :, :], 0.0, xn[:, :, :], ALU.min, ALU.subtract).then_inc(f_lf, 1)
                        dve.wait_ge(f_lf, 1)
                        for t in range(NT):
                            TT(lf_rows(t), each(ones, 8), spread(xa[:, t, :], 8), ALU.mult).then_inc(f_lf, 1)
                    if k == 12:
                        dve.wait_ge(f_mm, 1)
                        dve.tensor_copy(gam[:, :, :], ps[:, 7, 0:16].rearrange("p (t c) -> p t c", t=NT)
                                        ).then_inc(f_copied, 1)
                if p.kind == "k2" and p.j == 0 and k in (5, 8, 11, 14):
                    m = (k - 5) // 3
                    dve.wait_ge(f_mm, m + 2)
                    dve.tensor_copy(cum_row[:, 2 * m:2 * m + 2, :], halves(6 + m % 2)).then_inc(f_copied, 1)
                if p.kind in ("k2", "q2") and k == 7:
                    for c in range(2):
                        dve.wait_ge(turned, p.t0 + c + 1)
                        dst = (kT2 if p.kind == "k2" else qT2)[:, 4 * p.j + 2 * c:4 * p.j + 2 * c + 2, :]
                        dve.tensor_copy(dst, halves(4 + c)).then_inc(pt_read, 1)
                if p.kind in ("v2", "cc", "cb", "pu") and k == 3:
                    finished(p)
                    if p.kind == "cc":
                        dve.wait_ge(f_mm, 5)
                    for t in range(NT):
                        dst = {"v2": lambda: v2[:, t, BLK * p.j:BLK * (p.j + 1)], "cc": lambda: ccn[:, t, :],
                               "cb": lambda: ccn[:, t, :], "pu": lambda: pun[:, t, :]}[p.kind]()
                        TS(dst, acc(p, t), rstd[:, 4, t:t + 1], None, ALU.mult).then_inc(evac_dve, 1)
                if p.kind == "ch":
                    if k == 3:
                        finished(p)
                        dve.wait_ge(turned, p.t0)
                        dve.wait_ge(evac_dve, p.prev.n_dve)
                        for t in range(NT):
                            STT(hb[:, t, :], acc(p, t), rstd[:, 4, t:t + 1], ccn[:, t, :], ALU.mult,
                                ALU.mult).then_inc(evac_dve, 1)
                    if k in (7, 9, 11, 13):
                        j = (k - 7) // 2
                        dve.wait_ge(turned, p.t0 + j // 2 + 1)
                        conv(j, 3, COL["conv2"], 4, halves(4 + j // 2)[:, j % 2, :], ycT[:, j, :], yc_conv, j % 2 == 1)
                if p.kind == "gc":
                    if k == 4:
                        dve.wait_ge(evac_act, p.n_act)
                        dve.wait_ge(evac_dve, by["cb"][0].n_dve)
                        dve.wait_ge(turned, p.t0)
                        for t in range(NT):
                            TT(hb[:, t, :], gs[:, t, :], ccn[:, t, :], ALU.mult).then_inc(gated, 1)
                    if k == 7:
                        dve.wait_ge(yc_conv, 4)
                        for c in range(2):
                            dve.wait_ge(turned, p.t0 + c + 1)
                            link(TT(ycT[:, 2 * c:2 * c + 2, :], halves(4 + c), ycT[:, 2 * c:2 * c + 2, :], ALU.mult))
                            dve.sem_inc(pt_read, 1)
                            dve.sem_inc(yc_ready, 1)
                    if k == 9:
                        dve.wait_ge(yc_hi, 1)
                        TT(fl[:, 8:12, :], ycT[:, :, :], fh[:, 8:12, :].bitcast(F32), ALU.subtract).then_inc(yc_lo, 1)
                if p.kind == "gp" and k == 7:
                    for c in range(2):
                        dve.wait_ge(turned, p.t0 + c + 1)
                        dve.tensor_copy(spT[:, 2 * c:2 * c + 2, :], halves(4 + c)).then_inc(pt_read, 1)
                if p.kind == "final" and k == 3:
                    dve.wait_ge(mm_done, p.k0 + p.nk)
                    dve.wait_ge(x_out, 4)
                    for t in range(NT):
                        hs = h[:, t, BLK * p.j:BLK * (p.j + 1)]
                        STT(hs, hs, ALPHA, acc(p, t), ALU.mult, ALU.add).then_inc(evac_dve, 1)

            def low_f(p):
                for c in range(2):
                    dve.wait_ge(turned_hi, p.h0 + c + 1)
                    kt = bass.ds(p.fkt + 2 * c, 2)
                    TT(fl[:, kt, :], halves(4 + c), fh[:, kt, :].bitcast(F32), ALU.subtract).then_inc(pt_read, 1)

            def minus_abs():
                link(TS(xn[:, :, :], xa[:, :, :], -1.0, None, ALU.mult))
                ins = TT(xn[:, :, :], xn[:, :, :], xa[:, :, :], ALU.min)
                return ins

            def during(blk, k):
                if blk.kind == "v" and blk.j == 1 and k == 6:
                    dve.wait_ge(ws_turned, 1)
                    TT(wsT[:, :, :], quarters(6, 2), each(upper, 8), ALU.mult).then_inc(ws_ready, 1)
                if blk.b in heads_in:
                    n = heads_in[blk.b]
                    if k == 5:
                        dve.wait_ge(f_copied, 5)
                        if n:
                            dve.wait_ge(h_pt, n)
                        link(STT(hd_s[:, 0:P], cum_row[:, n, 0:P], gam[:, 0, n:n + 1], m_causal, ALU.subtract, ALU.subtract))
                        link(TS(hd_s[:, P:2 * P], cum_row[:, n, 0:P], gam[:, 1, n:n + 1], None, ALU.subtract))
                        link(STT(hd_s[:, 2 * P:3 * P], cum_row[:, n, P:2 * P], gam[:, 1, n:n + 1], m_causal,
                                 ALU.subtract, ALU.subtract))
                        dve.wait_ge(h_scored, n + 1)
                        link(STT(hd_s[:, :], ps[:, 6, 0:3 * P], B_HD ** -0.5, hd_s[:, :], ALU.mult, ALU.subtract))
                        link(dve.tensor_reduce(f_nm[:, 0:1], head_rows(0), AX.X, ALU.max, negate=True))
                        dve.tensor_reduce(f_nm[:, 1:2], head_rows(1), AX.X, ALU.max, negate=True).then_inc(h_nm, 1)
                    if k == 12:
                        dve.wait_ge(h_exp, 2 * (n + 1))
                        link(dve.reciprocal(f_rd, f_sm))
                        dve.wait_ge(h_pv, n + 1)
                        dve.wait_ge(evac_act, by["ga"][n // 4].n_act)
                        if n:
                            dve.wait_ge(h_yt, n)
                        for t in range(NT):
                            STT(ya[:, t, :], ps[:, 6, P * t:P * (t + 1)], f_rd[:, t:t + 1],
                                sga[:, t, P * n:P * (n + 1)], ALU.mult, ALU.mult).then_inc(h_ya, 1)
                    if k == 15:
                        dve.wait_ge(h_hi, n + 1)
                        TT(fl[:, n, :], ps[:, 7, 0:SEQ], fh[:, n, :].bitcast(F32), ALU.subtract).then_inc(h_lo, 1)
                if blk.kind == "final" and blk.j == 0:
                    if k == 5:
                        dve.wait_ge(z_mm, 1)
                        for c in range(2):
                            dve.tensor_copy(zT[:, 2 * c:2 * c + 2, :], halves(6 + c)).then_inc(z_copied, 1)
                    if k == 8:
                        dve.wait_ge(pw_mm, 1)
                        dve.wait_ge(pt_read, by["gp"][0].t0 + 2)
                        dve.wait_ge(turned, by["gc"][0].t0 + 2)
                        for g in range(4):
                            c = COL["pool_scale"] + g
                            STT(pooled[:, g, :], halves(6 + g // 2)[:, g % 2, :], cols[:, c:c + 1], spT[:, g, :],
                                ALU.mult, ALU.mult).then_inc(yp_ready, 1)
                    if k == 11:
                        dve.wait_ge(yp_hi, 1)
                        TT(fl[:, 12:16, :], pooled, fh[:, 12:16, :].bitcast(F32), ALU.subtract).then_inc(yp_lo, 1)
                    if k in (12, 13, 14, 15):
                        dve.wait_ge(gf_loaded, 16)
                        t, c = (k - 12) // 2, slice(1024 * (k % 2), 1024 * (k % 2 + 1))
                        STT(h[:, t, c], h[:, t, c], rstd[:, 4, t:t + 1], gf_row[:, c], ALU.mult,
                            ALU.mult).then_inc(x_out, 1)

            def stream(blk, p):
                for k, slot, kk, gi in k_slots(blk):
                    dve.wait_ge(hi_ready, blk.k0 + k + 1)
                    w = blk.width
                    TT(w_lo[:, k % 4, 0:w], raw[:, slot, kk, 0:w], w_hi[:, k % 4, 0:w].bitcast(F32),
                       ALU.subtract).then_inc(lo_ready, 1)
                    if p is not None:
                        after(p, k, blk)
                    during(blk, k)

            def mix():
                dve.wait_ge(evac_dve, by["qa"][1].n_dve)
                dve.wait_ge(mm_done, by["z"][1].k0 + KT)
                for t in range(NT):
                    for g in range(2):
                        src = att[:, t, A_Q + 64 * g:A_Q + 64 * (g + 1)]
                        ins = dve.tensor_copy(kd2[:, t, g, :].rearrange("p (b d) -> p b d", b=2), each(src, 2))
                    ins.then_inc(kd_ready, 1)
                dve.wait_ge(small_loaded, 80)
                link(TS(n_sinks, sinks, -1.0, None, ALU.mult))
                link(TT(xa[:, :, :], xa[:, :, :], each(dt_bias, NT), ALU.add))
                minus_abs().then_inc(g_in, 1)

                def pick(v, grp):
                    return v[:, 4 * grp:4 * grp + 4].rearrange("p (a b) -> p b a", b=2)

                for u in range(9):
                    if u < 8:
                        grp, t = u % 4, u // 4
                        w = P * (t + 1)
                        dve.wait_ge(scored, u + 1)
                        if u >= 2:
                            dve.wait_ge(p_turned, u - 1)
                        mask = m_causal if t == 0 else m_window
                        for b in range(2):
                            dst = e_s[:, u % 2, 2 * w * b:2 * w * (b + 1)].rearrange("p (i c) -> p i c", i=2)
                            src = ps[:, 2 * (u % 2) + b, 0:2 * w].rearrange("p (i c) -> p i c", i=2)
                            link(STT(dst, src, A_HD ** -0.5, each(mask, 2), ALU.mult, ALU.add))
                        nm = e_nm[:, u % 2, :].rearrange("p (b a) -> p b a", b=2)
                        es = e_es[:, u % 2, :].rearrange("p (b a) -> p b a", b=2)
                        link(dve.tensor_reduce(e_nm[:, u % 2, :],
                                               e_s[:, u % 2, 0:4 * w].rearrange("p (i c) -> p i c", i=4),
                                               AX.X, ALU.max, negate=True))
                        link(TT(nm, nm, pick(n_sinks, grp), ALU.min))
                        TT(es, nm, pick(sinks, grp), ALU.add).then_inc(a_nm, 1)
                    if u >= 1:
                        v = u - 1
                        grp, t = v % 4, v // 4
                        dve.wait_ge(a_exp_done, v + 1)
                        if v:
                            dve.wait_ge(a_out, v)
                        link(TT(e_rd, e_sm[:, v % 2, :], e_es[:, v % 2, :], ALU.add))
                        link(dve.reciprocal(e_rd, e_rd))
                        dve.wait_ge(pv_done, v + 1)
                        for b in range(2):
                            dst = att[:, t, 256 * grp:256 * (grp + 1)].rearrange("p (a b d) -> p b a d", a=2, b=2)[:, b]
                            src = ps[:, 6 + v % 2, P * b:P * (b + 1)].rearrange("p (a d) -> p a d", a=2)
                            ins = TT(dst, src, spread(e_rd[:, 2 * b:2 * b + 2], 2, 64), ALU.mult)
                        ins.then_inc(a_out, 1)
                dve.wait_ge(g_act, 1)
                link(STT(xa[:, :, :], xa[:, :, :], 0.0, xn[:, :, :], ALU.max, ALU.add))
                STT(g_log[:, :, :], xa[:, :, :], -1.0, each(a_exp, NT), ALU.mult, ALU.mult).then_inc(g_ready, 1)
                link(TS(beta[:, :, :], beta[:, :, :], 1.0, None, ALU.add))
                link(dve.reciprocal(beta[:, :, :], beta[:, :, :]))
                for n in range(4):
                    dve.wait_ge(l2_sq, n + 1)
                    dve.tensor_reduce(l2_ss[:, n // 2, n % 2, :], (dD, dE)[n % 2][:, :, :], AX.X,
                                      ALU.add).then_inc(l2_ms, 1)
                dve.wait_ge(l2_ms, 4)
                TS(l2_ss[:, :, :, :], l2_ss[:, :, :, :], EPS, None, ALU.add).then_inc(l2_ms, 1)
                dve.wait_ge(l2_rs, 1)
                for t in range(NT):
                    TT(heads(kn[:, t, :]), heads(kn[:, t, :]), spread(l2_r[:, 1, t, :], 8), ALU.mult).then_inc(l2_k, 1)
                for t in range(NT):
                    tok = slice(P * t, P * (t + 1))
                    if t:
                        dve.wait_ge(de_mm, 2 * LEVELS)
                    dve.wait_ge(g_ready, 1)
                    TT(dC[:, :, :], each(upper, 8), spread(g_log[:, t, :], 8), ALU.mult).then_inc(ug_ready, 1)
                    dve.wait_ge(gam_mm, t + 1)
                    link(dve.tensor_copy(gam[:, t, :], ps[:, 4, 0:8]))
                    if t == 0:
                        link(TT(k_scale[:, 0, :], quarters(0, 2)[:, :, P - 1], gam[:, 0, :], ALU.subtract))
                    dve.sem_inc(gam_ready, 1)
                    if t == 1:
                        dve.wait_ge(q_scale, 1)
                    link(TT(dY[:, :, :], quarters(0, 2), spread(gam[:, t, :], 8), ALU.subtract))
                    link(TS(dC[:, :, :], dY[:, :, :], 0.0, None, ALU.min))
                    TS(dY[:, :, :], dY[:, :, :], 0.0, None, ALU.max).then_inc(dec_in, 1)
                    dve.wait_ge(dec_exp, t + 1)
                    link(TT(dL[:, :, :], dL[:, :, :], each(strict, 8), ALU.mult))
                    link(TT(dQK[:, :, :], dQK[:, :, :], each(upper, 8), ALU.mult))
                    dve.wait_ge(kq_mm, t + 1)
                    link(TT(dL[:, :, :], quarters(2, 2), dL[:, :, :], ALU.mult))
                    link(TT(dL[:, :, :], dL[:, :, :], spread(beta[:, t, :], 8), ALU.mult))
                    TT(dQK[:, :, :], quarters(6, 2), dQK[:, :, :], ALU.mult).then_inc(lqk_ready, 1)
                    dve.wait_ge(c_ready, LEVELS * t + 1)
                    for half in range(2):
                        four = slice(4 * half, 4 * half + 4)
                        TT(dD[:, four, :], each(ident, 4), dC[:, four, :], ALU.subtract)
                        dve.wait_ge(de_mm, 2 * LEVELS * t + half + 1)
                        TT(dE[:, four, :], each(ident, 4), quarters(4 + half), ALU.subtract).then_inc(de_ready, 1)
                    for lv in range(1, LEVELS):
                        if lv == 1:
                            TT(heads(vn[:, t, :]), heads(vn[:, t, :]), spread(beta[:, t, :], 8), ALU.mult)
                            scale = k_scale[:, 0, :]
                            if t == 1:
                                link(TT(k_scale[:, 1, :], beta[:, 1, :], e_gam[:, 1, :], ALU.mult))
                                scale = k_scale[:, 1, :]
                                TT(q_dec[:, :, :], q_dec[:, :, :], dqT[:, :, tok], ALU.mult)
                            TT(dkb[:, :, :], heads(kn[:, t, :]), spread(scale, 8), ALU.mult).then_inc(kv_ready, 1)
                        for half in range(2):
                            four = slice(4 * half, 4 * half + 4)
                            dve.wait_ge(de_mm, 2 * (LEVELS * t + lv) + half + 1)
                            dve.wait_ge(de_ready, 2 * (LEVELS * t + lv - 1) + half + 1)
                            if lv < LEVELS - 1:
                                TT(dD[:, four, :], dD[:, four, :], quarters(2 + half), ALU.subtract)
                            TT(dE[:, four, :], dE[:, four, :], quarters(4 + half), ALU.subtract).then_inc(de_ready, 1)
                    dve.wait_ge(u_mm, t + 1)
                    dve.tensor_copy(v_new[:, :, :], quarters(0, 2)).then_inc(vnew_ready, 1)
                    dve.wait_ge(o_sq, t + 1)
                    link(dve.tensor_reduce(o_ss, dD[:, :, :], AX.X, ALU.add))
                    TS(o_ss, o_ss, 1.0 / B_HD, EPS, ALU.mult, ALU.add).then_inc(o_ms, 1)
                    dve.wait_ge(o_rs, t + 1)
                    dst = heads(qn[:, t, :])
                    link(TT(dst, quarters(4, 2), spread(o_r, 8), ALU.mult))
                    link(TT(dst, dst, each(onorm, 8), ALU.mult))
                    dve.wait_ge(evac_act, by["z"][1].n_act)
                    TT(dst, dst, heads(zs[:, t, :]), ALU.mult).then_inc(o_done, 1)
                for m in range(T_INIT):
                    dve.wait_ge(turned_hi, even_resid[0].h0 - T_INIT + m + 1)
                    TT(fl[:, 2 * m:2 * m + 2, :], halves(4 + m % 2), fh[:, 2 * m:2 * m + 2, :].bitcast(F32),
                       ALU.subtract).then_inc(pt_read, 1)

            run_blocks(dve, stream, mix)
            after(blocks[-1], 3, None)
            dve.wait_ge(r_stat, 8)
            link(dve.tensor_reduce(v_mu, v_sum[:, :, :], AX.X, ALU.add))
            link(TS(v_mu, v_mu, 1.0 / D, None, ALU.mult))
            TS(v_nmu, v_mu, -1.0, None, ALU.mult).then_inc(r_stat, 1)
            dve.wait_ge(ln2_loaded, 32)
            for t in range(NT):
                link(STT(fin[:, t, :], h[:, t, :], v_mu[:, t:t + 1], ln2_g_row[:, :], ALU.subtract, ALU.mult))
            dve.wait_ge(r_sq, 2)
            TS(v_var, v_var, 1.0 / D, LN2_EPS, ALU.mult, ALU.add).then_inc(r_ms, 1)
            dve.wait_ge(r_rs, 1)
            for n in range(4):
                t, c = n // 2, slice(1024 * (n % 2), 1024 * (n % 2 + 1))
                STT(fin[:, t, c], fin[:, t, c], v_rstd[:, t:t + 1], ln2_b_row[:, c], ALU.mult,
                    ALU.add).then_inc(fin_ready, 1)

        @block.gpsimd
        def _(gp):
            gp.memset(neg_half, -0.5).then_inc(pool_init, 1)
            gp.wait_ge(pool_init, 1)

            def inverse_root(dst, src, n, wait, value, done):
                gp.wait_ge(wait, value)
                gp.tensor_tensor(dst, src, neg_half[:, 0:n], ALU.pow).then_inc(done, 1)

            inverse_root(rstd[:, 0, :], ms, 2, ms_ready, 1, rstd_ready)
            gp.wait_ge(l2_ms, 5)
            flat = "p x t h -> p (x t h)"
            gp.tensor_tensor(l2_r.rearrange(flat), l2_ss.rearrange(flat), neg_half, ALU.pow).then_inc(l2_rs, 1)
            gp.wait_ge(l2_rs, 1)
            gp.tensor_scalar(l2_q_r, l2_r[:, 0, :, :], B_HD ** -0.5, None, ALU.mult).then_inc(l2_rs, 1)
            gp.wait_ge(l2_rs, 2)
            for t in range(NT):
                q = qn[:, t, :].rearrange("p (h c) -> p h c", h=8)
                gp.tensor_tensor(q, q, l2_q_r[:, t, :].unsqueeze(2).to_broadcast([P, 8, P]), ALU.mult).then_inc(l2_q, 1)
            for t in range(NT):
                for lv in range(LEVELS):
                    if lv == 0:
                        gp.wait_ge(masks_loaded, 16)
                        gp.wait_ge(lqk_ready, t + 1)
                    elif lv == 1:
                        gp.wait_ge(de_ready, 2 * LEVELS * t + 2)
                    else:
                        gp.wait_ge(y_mm, 2 * ((LEVELS - 1) * t + lv - 1))
                    gp.tensor_tensor(dC[:, :, :], dL[:, :, :], masks[:, lv, :].unsqueeze(1).to_broadcast([P, 8, P]),
                                     ALU.mult).then_inc(c_ready, 1)
                inverse_root(o_r, o_ss, 8, o_ms, t + 1, o_rs)
            inverse_root(rstd[:, 1, :], ms, 2, ms_ready, 2, rstd_ready)
            inverse_root(rstd[:, 2, :], ms, 2, ms_ready, 3, rstd_ready)
            inverse_root(v_rstd, v_var, 2, v_ms, 1, v_rs)
            inverse_root(rstd[:, 3, :], ms, 2, ms_ready, 4, rstd_ready)
            inverse_root(rstd[:, 4, :], ms, 2, ms_ready, 5, rstd_ready)
            inverse_root(v_rstd, v_var, 2, r_ms, 1, r_rs)


_INS = ["x", "even_norm", "even_w_in", "even_conv", "even_a_log", "even_dt_bias", "even_sinks", "even_onorm",
        "even_w_out", "odd_norm", "odd_w_in", "odd_ln_g", "odd_ln_b", "odd_w_s", "odd_b_s", "odd_w_out", "ffn_norm",
        "ffn_w_gate", "ffn_w_up", "ffn_w_down", "final_norm", "w_in_2", "b_f_2", "conv_w_2", "pool_w_2",
        "pool_scale_2", "w_out_2", "ln_g_2", "ln_b_2"]


def kernel(**inputs):
    import numpy as _np
    import concourse.bacc as _bacc
    from concourse import mybir as _mybir
    from concourse.bass_utils import run_bass_kernel_spmd as _run

    nc = _bacc.Bacc("TRN2", target_bir_lowering=False, num_devices=1)
    arrays, aps = {}, {}
    squeeze = ("even_w_in", "even_w_out", "odd_w_in", "odd_w_out", "w_in_2", "w_out_2")
    for name in _INS:
        v = _np.ascontiguousarray(inputs[name])
        arrays[f"in_{name}"] = v[0] if name in squeeze else v
    arrays["in_consts"], arrays["in_pool_consts"] = shape_constants()
    for key, v in arrays.items():
        aps[key[3:]] = nc.dram_tensor(key, v.shape, _mybir.dt.from_np(v.dtype), kind="ExternalInput").ap()
    out = nc.dram_tensor("out_0", (1, SEQ, D), _mybir.dt.float32, kind="ExternalOutput").ap()
    program(nc, aps, out)
    return _run(nc, [arrays], core_ids=[0]).results[0]["out_0"]
```

```python
from contextlib import ExitStack

import numpy as np

import concourse.bass as bass
from concourse import mybir

ACT = mybir.ActivationFunctionType
ALU = mybir.AluOpType
AX = mybir.AxisListType
F32 = mybir.dt.float32
F32R = mybir.dt.float32r

P = 128
D = 2048
SEQ = 256
RING = 8
NT = SEQ // P
KT = D // P
BLK = 512
DFF = 5632
FKT = DFF // P
NPAIR = DFF // BLK
EPS = 1e-6
LN2_EPS = 1e-5
ALPHA = 2.0 ** 0.25
A_Q, A_KV, A_HD = 1024, 128, 64
B_HEADS, B_HD = 8, 128
NEG = -1e30

C_IDENT, C_UPPER, C_ONES, C_PREV, C_CAUSAL, C_LEVEL = [P * i for i in range(6)]
LEVELS = 7
N_CONST = C_LEVEL + LEVELS * P
POOL_WINDOWS = (2, 4, 8, 16)


def shape_constants():
    i = np.arange(P)[:, None]
    j = np.arange(P)[None, :]
    f = np.float32
    parts = [
        (i == j).astype(f), (i <= j).astype(f), np.ones((P, P), f),
        np.where(j > i, 0.0, NEG).astype(f),
        np.where(j <= i, 0.0, NEG).astype(f),
    ]
    for level in range(LEVELS):
        s = 1 << level
        parts.append(((i // (2 * s) == j // (2 * s)) & (i // s > j // s)).astype(f))
    consts = np.concatenate(parts, axis=1)
    s = np.arange(SEQ)[:, None]
    t = np.arange(SEQ)[None, :]
    pool = np.stack([((t - s >= 0) & (t - s < w)) / np.minimum(t + 1.0, float(w)) - (s == t)
                     for w in POOL_WINDOWS], axis=1).astype(f)
    return consts, pool


ROWS_A = (("even_norm", 16), ("ffn0_norm", 16), ("ffn1_norm", 16), ("odd_norm", 16),
          ("final_norm", 16), ("pool_scale", 4), ("conv2", 12), ("b_s", 8))
COL = {}
_at = 0
for _n, _r in ROWS_A:
    COL[_n] = _at
    _at += _r
N_ROWS_A = _at
COL["conv"] = _at
N_ROWS_B = 96
N_COLS = N_ROWS_A + N_ROWS_B
NORMS = ("even_norm", "ffn0_norm", "odd_norm", "ffn1_norm", "final_norm")


class Block:

    def __init__(self, kind, j, pieces, width, nk=KT, lhs="x", kt0=0):
        self.kind, self.j, self.pieces, self.width, self.nk, self.lhs = kind, j, pieces, width, nk, lhs
        self.kt0 = kt0
        self.groups = [2] * (nk // 2)


ACT_KINDS = ("z", "gate", "v", "u", "ga", "gc", "gp")
SPLIT_KINDS = ("resid", "up", "u")
COPY_KINDS = ("conv", "k2", "q2", "ch", "gc", "gp")


T_INIT = KT // 2
PHASE = {"kvba": 0, "qa": 0, "conv": 0, "z": 0, "half": 6, "resid": 1, "gate": 2, "up": 2, "v": 3, "u": 3,
         "fg": 4, "k2": 4, "q2": 4, "v2": 4, "ga": 4, "cc": 4, "ch": 4, "cb": 4, "gc": 4, "pu": 4, "gp": 4,
         "final": 5}


def plan(w):
    out = []
    e = w["even_w_in"]
    kv = A_Q
    out += [Block("conv", j, [(e, 1280 + BLK * j, BLK, 0)], BLK) for j in range(6)]
    out.append(Block("kvba", 0, [(e, kv, 256, 0), (e, 5376, 16, 256)], 272))
    out += [Block("z", j, [(e, 4352 + BLK * j, BLK, 0)], BLK) for j in range(2)]
    out += [Block("qa", j, [(e, BLK * j, BLK, 0)], BLK) for j in range(2)]
    half = KT // 2
    out += [Block("half", j, [(w["even_w_out"], BLK * j, BLK, 0)], BLK, nk=half, lhs="f", kt0=half)
            for j in range(4)]
    out += [Block("resid", j, [(w["even_w_out"], BLK * j, BLK, 0)], BLK, nk=half, lhs="f") for j in range(4)]

    def ffn(n):
        for i in range(NPAIR):
            out.append(Block("gate", i, [(w[f"gate{n}"], BLK * i, BLK, 0)], BLK))
            out.append(Block("up", i, [(w[f"up{n}"], BLK * i, BLK, 0)], BLK))
        for j in range(4):
            out.append(Block("resid", j, [(w[f"down{n}"], BLK * j, BLK, 0)], BLK, nk=FKT, lhs="f"))

    ffn(0)
    o = w["odd_w_in"]
    out.extend(Block("v", j, [(o, D + BLK * j, BLK, 0)], BLK) for j in range(4))
    out.extend(Block("u", j, [(o, BLK * j, BLK, 0)], BLK) for j in range(4))
    out.extend(Block("resid", j, [(w["odd_w_out"], BLK * j, BLK, 0)], BLK, lhs="f") for j in range(4))
    ffn(1)
    s = w["w_in_2"]
    for kind, j, c, n in (("fg", 0, 4096, 8), ("k2", 0, 1024, BLK), ("q2", 0, 0, BLK), ("v2", 0, 2048, BLK),
                          ("ga", 0, 3072, BLK), ("k2", 1, 1536, BLK), ("q2", 1, BLK, BLK), ("v2", 1, 2560, BLK),
                          ("ga", 1, 3584, BLK), ("cc", 0, 4616, BLK), ("ch", 0, 5128, BLK), ("cb", 0, 4104, BLK),
                          ("gc", 0, 5640, BLK), ("pu", 0, 6152, BLK), ("gp", 0, 6664, BLK)):
        out.append(Block(kind, j, [(s, c, n, 0)], n))
    out.extend(Block("final", j, [(w["w_out_2"], BLK * j, BLK, 0)], BLK, lhs="f") for j in range(4))

    g = k = norm = n_act = n_dve = 0
    t, s = T_INIT, T_INIT
    mix_t0 = mix_h0 = None
    ends = []
    for b, blk in enumerate(out):
        if blk.kind == "half" and blk.j == 0:
            mix_t0, mix_h0 = t, s
            t, s = t + T_INIT, s + T_INIT
        if norm == 0:
            blk.mix_t0, blk.mix_h0 = mix_t0, mix_h0
        blk.b, blk.g0, blk.k0, blk.t0, blk.h0, blk.norm = b, g, k, t, s, norm
        blk.prev = out[b - 1] if b else None
        blk.fkt = 4 * blk.j
        blk.first = not b or PHASE[out[b - 1].kind] != PHASE[blk.kind]
        blk.slot0, blk.uses, blk.ring = g % 4, g // 4, k % RING
        g += len(blk.groups)
        for n in blk.groups:
            k += n
            ends.append(k)
        blk.by_act = blk.kind in ACT_KINDS
        n_act += NT * blk.by_act
        n_dve += NT * (not blk.by_act)
        blk.n_act, blk.n_dve = n_act, n_dve
        t += 2 * (blk.kind in SPLIT_KINDS + COPY_KINDS)
        s += 2 * (blk.kind in SPLIT_KINDS)
        norm += blk.kind == "resid" and blk.j == 3
    return out, ends


class Later:

    def __init__(self, blk, it):
        self.kind, self.j, self.b, self.width, self.nk, self.lhs = blk.kind, blk.j, blk.b, blk.width, blk.nk, blk.lhs
        self.norm, self.groups, self.first, self.by_act = blk.norm, blk.groups, False, blk.by_act
        self.g0, self.k0, self.ring = blk.g0 + 16 * it, blk.k0 + 32 * it, blk.ring
        self.slot0, self.uses, self.kt0 = blk.slot0, blk.uses + 4 * it, 0
        self.n_act, self.n_dve = blk.n_act + 2 * it, blk.n_dve + 2 * it
        self.t0, self.h0 = blk.t0 + 2 * it, blk.h0 + 2 * it
        self.fkt = 4 * it + 4 * blk.j
        self.cols = BLK * it


def program(nc, a, out):
    weights = {n: a[n].rearrange("(k p) n -> p k n", p=P) for n in (
        "even_w_in", "even_w_out", "odd_w_in", "odd_w_out", "w_in_2", "w_out_2")}
    for n in range(2):
        for key in ("gate", "up", "down"):
            weights[f"{key}{n}"] = a[f"ffn_w_{key}"][n].rearrange("(k p) n -> p k n", p=P)
    blocks, group_ends = plan(weights)
    by = {}
    for blk in blocks:
        by.setdefault(blk.kind, []).append(blk)
    even_resid, ffn_resid = by["resid"][0:4], (by["resid"][4:8], by["resid"][12:16])
    odd_resid = by["resid"][8:12]
    pairs = [[(by["gate"][n * NPAIR + i], by["up"][n * NPAIR + i]) for i in range(NPAIR)] for n in range(2)]
    heads_in = {blk.b: n for n, blk in enumerate(blocks[by["k2"][1].b:by["k2"][1].b + 8])}

    ctx = ExitStack()
    with ctx:
        def sem(name):
            return ctx.enter_context(nc.semaphore(name))

        def sb(name, shape, dt=F32):
            return ctx.enter_context(nc.sbuf_tensor(name, shape, dt))

        h = sb("h", [P, NT, D])
        raw = sb("raw", [P, 4, 2, BLK])
        w_hi = sb("w_hi", [P, RING, BLK], F32R)
        w_lo = sb("w_lo", [P, RING, BLK], F32R)
        gs = sb("gs", [P, NT, BLK])
        hb = sb("hb", [P, NT, BLK])
        consts = sb("consts_sb", [P, C_LEVEL])
        cols = sb("cols", [P, N_COLS])
        small = sb("small", [P, 168])
        stat = sb("stat", [P, 408])
        extra = sb("extra", [P, 8, SEQ])

        ident = consts[:, C_IDENT:C_IDENT + P]
        upper = consts[:, C_UPPER:C_UPPER + P]
        upper_ones = consts[:, C_UPPER:C_UPPER + 2 * P]
        ones = consts[:, C_ONES:C_ONES + P]
        m_causal = consts[:, C_CAUSAL:C_CAUSAL + P]
        m_window = consts[:, C_PREV:C_PREV + 2 * P]
        dt_bias, a_log, sinks = small[:, 0:8], small[:, 8:16], small[:, 16:32]
        onorm, b_f = small[:, 32:160], small[:, 160:168]

        used = [0]

        def st(*shape):
            n = int(np.prod(shape))
            v = stat[:, used[0]:used[0] + n]
            used[0] += n
            assert used[0] <= 408
            if len(shape) == 2:
                return v.rearrange("p (x y) -> p x y", x=shape[0])
            if len(shape) == 3:
                return v.rearrange("p (x y z) -> p x y z", x=shape[0], y=shape[1])
            return v

        neg_half = st(32)
        ssq, ms, rstd = st(5, NT, 4), st(2), st(5, NT)
        v_sum, v_mu, v_nmu, v_var, v_rstd = st(NT, 4), st(2), st(2), st(2), st(2)
        e_nm, e_es, e_sm, e_rd = st(2, 4), st(3, 4), st(3, 4), st(4)
        n_sinks = st(16)
        l2_ss, l2_r = st(2, NT, 8), st(2, NT, 8)
        ba, xa, xn, beta, g_log, gam, e_gam, k_scale = [st(NT, 8) for _ in range(8)]
        a_exp = st(8)
        o_ss, o_r, l2_q_r = st(8), st(8), st(NT, 8)
        f_nm, f_sm, f_rd = st(2), st(2), st(2)

        def overlay(*parts):
            got = []
            with ExitStack() as shared:
                for name, shape, *dt in parts:
                    got.append(shared.enter_context(nc.sbuf_tensor(name, shape, dt[0] if dt else F32)))
            return got

        xh, xl, fh, fl = overlay(("xh", [P, KT, SEQ], F32R), ("xl", [P, KT, SEQ], F32R),
                                 ("fh", [P, FKT, SEQ], F32R), ("fl", [P, FKT, SEQ], F32R))
        kTa, qaT, e_s, e_pT, _, _, qkv, S1, _, att, zs, dqT = overlay(
            ("kTa", [P, 2, SEQ]), ("qaT", [P, 16, SEQ]), ("e_s", [P, 2, BLK]), ("e_pT", [P, 2, 4, P]),
            ("pad_e0", [P, 1536]), ("pad_e1", [P, 4096]), ("qkv", [P, 3, NT, 1024]), ("S1", [P, 8, P]),
            ("pad_e2", [P, 4096]), ("att", [P, NT, 1280]), ("zs", [P, NT, 1024]), ("dqT", [P, 8, SEQ]))
        _, dL, dQK, dD, dE, _, dY, dC, dkb, masks = overlay(
            ("pad_d0", [P, 8192]), *[(n, [P, 8, P]) for n in ("dL", "dQK", "dD", "dE")],
            ("pad_d1", [P, 28 * SEQ]), *[(n, [P, 8, P]) for n in ("dY", "dC", "dkb")],
            ("level_masks", [P, LEVELS, P]))
        _, v_nat, ln_g_row, wsT, _, mixed, ln_b_row, ws_nat = overlay(
            ("pad_o0", [P, 12288]), ("v_nat", [P, NT, D]), ("ln_g_row", [P, D]), ("wsT", [P, 8, P]),
            ("pad_o1", [P, 4096]), ("mixed", [P, NT, D]), ("ln_b_row", [P, D]), ("ws_nat", [P, 8, P]))
        _, kT2, qT2, v2, ycT, _, sga, pun, ccn, spT, hd_s, hd_pT, ya = overlay(
            ("pad_s0", [P, 12288]), ("kT2", [P, 8, SEQ]), ("qT2", [P, 8, SEQ]), ("v2", [P, NT, 1024]),
            ("ycT", [P, 4, SEQ]), ("pad_s1", [P, 4096]), ("sga", [P, NT, 1024]), ("pun", [P, NT, BLK]),
            ("ccn", [P, NT, BLK]), ("spT", [P, 4, SEQ]), ("hd_s", [P, 384]), ("hd_pT", [P, 3, P]),
            ("ya", [P, NT, P]))
        poolm, poolw, zT, gf_row = overlay(("poolm", [P, NT, 4, SEQ]), ("poolw", [P, 4, P]),
                                           ("zT", [P, 4, SEQ]), ("gf_row", [P, D]))
        fin, _, junk = overlay(("fin", [P, NT, D]), ("pad_j", [P, 4096]), ("junk", [P, D]))
        _, ln2_g_row, ln2_b_row = overlay(("pad_f0", [P, 12288]), ("ln2_g_row", [P, D]), ("ln2_b_row", [P, D]))
        conv_buf = gs[:, :, :].rearrange("p t (c n) -> p (t c) n", c=2)
        silu_buf = extra[:, 0:4, :]
        dkT = extra
        v_new = gs[:, :, :].rearrange("p t (c n) -> p (t c) n", c=4)
        q_dec = hb[:, :, :].rearrange("p t (c n) -> p (t c) n", c=4)
        cum_row = extra
        qn, kn, vn = qkv[:, 0], qkv[:, 1], qkv[:, 2]

        ps = ctx.enter_context(nc.psum_tensor("ps", [P, 8, BLK], F32))

        pooled = hb[:, :, :].rearrange("p t (c n) -> p (t c) n", c=2)

        def acc(blk, t):
            return ps[:, 2 * (blk.b % 2) + t, 0:blk.width]

        def halves(bank):
            return ps[:, bank, :].rearrange("p (k c) -> p k c", k=2)

        def quarters(first, n=1):
            return ps[:, first:first + n, :].rearrange("p b (k c) -> p (b k) c", k=4)

        x_loaded, const_loaded, rows_loaded, small_loaded = [sem(n) for n in (
            "x_loaded", "const_loaded", "rows_loaded", "small_loaded")]
        raw_ready = [sem(f"raw_ready{i}") for i in range(4)]
        hi_ready, lo_ready, mm_done = sem("hi_ready"), sem("lo_ready"), sem("mm_done")
        evac_act, evac_dve = sem("evac_act"), sem("evac_dve")
        turned, turned_hi, pt_read = sem("turned"), sem("turned_hi"), sem("pt_read")
        sq_done, ms_ready, rstd_ready = sem("sq_done"), sem("ms_ready"), sem("rstd_ready")
        pool_init, cols_t, cols_ready, dve_link, act_link = [sem(n) for n in (
            "pool_init", "cols_t", "cols_ready", "dve_link", "act_link")]
        conv_done, conv_silu, back_t, back_copied = [sem(n) for n in (
            "conv_done", "conv_silu", "back_t", "back_copied")]
        masks_loaded, a_turned, a_copied = [sem(n) for n in (
            "masks_loaded", "a_turned", "a_copied")]
        scored, a_nm, a_exp_done, p_turned, p_copied, pv_done, a_out = [sem(n) for n in (
            "scored", "a_nm", "a_exp_done", "p_turned", "p_copied", "pv_done", "a_out")]
        l2_sq, l2_ms, l2_rs, l2_q, l2_k, d_turned, d_copied = [sem(n) for n in (
            "l2_sq", "l2_ms", "l2_rs", "l2_q", "l2_k", "d_turned", "d_copied")]
        g_in, g_act, g_ready, ug_ready, gam_mm, gam_ready = [sem(n) for n in (
            "g_in", "g_act", "g_ready", "ug_ready", "gam_mm", "gam_ready")]
        dec_in, dec_exp, kq_mm, lqk_ready, kv_ready = [sem(n) for n in (
            "dec_in", "dec_exp", "kq_mm", "lqk_ready", "kv_ready")]
        c_ready, y_mm, y_copied, de_mm, de_ready = [sem(n) for n in (
            "c_ready", "y_mm", "y_copied", "de_mm", "de_ready")]
        w_mm, w_copied, u_mm, vnew_ready, s_mm, s_ready, o_mm = [sem(n) for n in (
            "w_mm", "w_copied", "u_mm", "vnew_ready", "s_mm", "s_ready", "o_mm")]
        q_scale = sem("q_scale")
        o_sq, o_ms, o_rs, o_done = [sem(n) for n in ("o_sq", "o_ms", "o_rs", "o_done")]
        ln_loaded, ws_turned, ws_ready, v_stat, v_sq, v_ms, v_rs, v_done = [sem(n) for n in (
            "ln_loaded", "ws_turned", "ws_ready", "v_stat", "v_sq", "v_ms", "v_rs", "v_done")]
        mix_mm, mix_out, gated = sem("mix_mm"), sem("mix_out"), sem("gated")
        f_in, f_act, f_lf, f_mm, f_copied = [sem(n) for n in ("f_in", "f_act", "f_lf", "f_mm", "f_copied")]
        h_scored, h_nm, h_exp, h_pt, h_ptc, h_pv, h_ya, h_yt, h_hi, h_lo = [sem(n) for n in (
            "h_scored", "h_nm", "h_exp", "h_pt", "h_ptc", "h_pv", "h_ya", "h_yt", "h_hi", "h_lo")]
        yc_conv, yc_ready, yc_hi, yc_lo = sem("yc_conv"), sem("yc_ready"), sem("yc_hi"), sem("yc_lo")
        pool_loaded, z_mm, z_copied, pw_mm, yp_ready, yp_hi, yp_lo = [sem(n) for n in (
            "pool_loaded", "z_mm", "z_copied", "pw_mm", "yp_ready", "yp_hi", "yp_lo")]
        gf_loaded, ln2_loaded, x_out, r_stat, r_sq, r_ms, r_rs, fin_ready, stored = [sem(n) for n in (
            "gf_loaded", "ln2_loaded", "x_out", "r_stat", "r_sq", "r_ms", "r_rs", "fin_ready", "stored")]

        def k_slots(blk):
            k = 0
            for gi, n in enumerate(blk.groups):
                g = blk.slot0 + gi
                kvba = by["kvba"][0].b
                two_loads = 0 if blk.b < kvba else gi // 4 + 1 if blk.b == kvba else 2
                for kk in range(n):
                    yield k, g % 4, kk, blk.uses + g // 4 + 1 + two_loads
                    k += 1

        def run_blocks(eng, stream, delta=None, attention=None, lag=0):
            b = 0
            idle = iter(())
            while b < len(blocks):
                blk = blocks[b]
                if blk.kind == "gate" and blk.j == 1:
                    n = 0 if blk is pairs[0][1][0] else 1
                    gate, up = pairs[n][1]
                    last_up = pairs[n][0][1]
                    with eng.Fori(0, NPAIR - 1) as it:
                        g, u, lu = Later(gate, it), Later(up, it), Later(last_up, it)
                        stream(g, lu, idle, 0)
                        stream(u, g, idle, 0)
                    b += 2 * (NPAIR - 1)
                    continue
                if delta and blk is by["z"][0]:
                    mixer, start = delta(), 3 + lag
                if attention and blk is by["half"][0]:
                    for _ in mixer:
                        pass
                    mixer, start = attention(), 2 + lag
                if attention and blk is even_resid[0]:
                    for _ in mixer:
                        pass
                    mixer = idle
                if not delta or b < by["z"][0].b:
                    mixer, start = idle, 0
                stream(blk, blk.prev, mixer, start if blk is by["z"][0] or blk is by["half"][0] else 0)
                b += 1

        def linker(eng, s):
            n = [0]

            def link(ins):
                n[0] += 1
                ins.then_inc(s, 1)
                eng.wait_ge(s, n[0])
            return link

        def lf_rows(t):
            return (gs if t == 0 else ccn)[:, :, :].rearrange("p t (c n) -> p (t c) n", c=4)

        def head_rows(t):
            return hd_s[:, 0:P] if t == 0 else hd_s[:, P:3 * P]

        UNITS = [u for g in range(0, 16, 4) for u in ((0, g, 4), (1, g, 2), (1, g + 2, 2))]

        def y_bank(lv):
            return 4 if lv % 2 else 6

        def de_bank(lv, half):
            return y_bank(lv) if half else 10 - y_bank(lv)

        def u_hooks(blk):
            return (8, 9, 10, 13) if blk.j == 0 else (3, 3, 4, 7)

        block = ctx.enter_context(nc.Block())

        @block.sync
        def _(sp):
            sp.dma_start(consts[:], a["consts"][:, 0:C_LEVEL]).then_inc(const_loaded, 16)
            x_rows = a["x"].rearrange("b (t p) d -> p (b t) d", p=P)
            for t in range(NT):
                sp.dma_start(h[:, t, :], x_rows[:, t, :]).then_inc(x_loaded, 16)

            def load(blk, _prev, _mixer, _start):
                k = 0
                for gi, n in enumerate(blk.groups):
                    if isinstance(blk, Later):
                        sp.wait_ge(lo_ready, blk.k0 + k - 6)
                    elif blk.g0 + gi >= 4:
                        sp.wait_ge(lo_ready, group_ends[blk.g0 + gi - 4])
                    for w, col, width, at in pieces_of(blk):
                        slot = (blk.slot0 + gi) % 4
                        sp.dma_start(raw[:, slot, 0:n, at:at + width],
                                     w[:, blk.kt0 + k:blk.kt0 + k + n, bass.ds(col, width)]
                                     ).then_inc(raw_ready[slot], 16)
                    k += n

            def pieces_of(blk):
                if isinstance(blk, Later):
                    w, col, width, at = blocks[blk.b].pieces[0]
                    return [(w, col + blk.cols, width, at)]
                return blk.pieces

            run_blocks(sp, load)

        @block.scalar
        def _(act):
            link = linker(act, act_link)
            for name, n in ROWS_A:
                src = {"even_norm": a["even_norm"], "ffn0_norm": a["ffn_norm"][0:1], "ffn1_norm": a["ffn_norm"][1:2],
                       "odd_norm": a["odd_norm"], "final_norm": a["final_norm"], "pool_scale": a["pool_scale_2"],
                       "conv2": a["conv_w_2"], "b_s": a["odd_b_s"]}[name]
                pattern = {"final_norm": "(k c) -> k c", "conv2": "a t (k c) -> (a t k) c",
                           "b_s": "a k c -> (a k) c"}.get(name, "a (k c) -> (a k) c")
                kw = {} if name == "b_s" else {"c": P}
                act.dma_start(hb[COL[name]:COL[name] + n, 0, 0:P], src.rearrange(pattern, **kw)).then_inc(rows_loaded, 16)
            act.dma_start(hb[0:N_ROWS_B, 1, 0:P],
                          a["even_conv"].rearrange("a t (k c) -> (a t k) c", c=P)).then_inc(rows_loaded, 16)
            for dst, src, n in ((dt_bias, a["even_dt_bias"], 8), (a_log, a["even_a_log"], 8),
                                (sinks, a["even_sinks"], 16), (onorm, a["even_onorm"], P), (b_f, a["b_f_2"], 8)):
                act.dma_start(dst, src.to_broadcast([P, n])).then_inc(small_loaded, 16)
            def square(norm, j, t):
                n = 8 * norm + 2 * j + t if norm else 4 * t + j
                if n:
                    act.wait_ge(sq_done, n)
                act.activation(gs[:, t, :], h[:, t, BLK * j:BLK * (j + 1)], ACT.Square,
                               accum_out=ssq[:, norm, t, j:j + 1]).then_inc(sq_done, 1)

            act.dma_start(masks[:, :, :], a["consts"][:, C_LEVEL:N_CONST].rearrange("p (l c) -> p l c", l=LEVELS)
                          ).then_inc(masks_loaded, 16)
            act.wait_ge(x_loaded, 16 * NT)
            for t in range(NT):
                for j in range(4):
                    square(0, j, t)

            def split_x(gain, kt, c, t0, h0):
                act.wait_ge(turned, t0 + c + 1)
                for kk in range(2):
                    ins = act.activation(xh[:, kt + kk, :], halves(4 + c)[:, kk, :], ACT.Copy,
                                         scale=cols[:, gain + kt + kk:gain + kt + kk + 1])
                ins.then_inc(turned_hi, 1)

            act.wait_ge(cols_ready, 1)
            for m in range(T_INIT):
                split_x(COL["even_norm"], 2 * m, m % 2, m - m % 2, 0)

            def finished(p):
                act.wait_ge(mm_done, p.k0 + p.nk)

            def after(p, k, blk):
                if p.kind == "z" and k == 3:
                    finished(p)
                    for t in range(NT):
                        act.activation(zs[:, t, BLK * p.j:BLK * (p.j + 1)], acc(p, t), ACT.Silu,
                                       scale=rstd[:, 0, t:t + 1]).then_inc(evac_act, 1)
                if p.kind == "conv" and k in (8, 10, 12, 14):
                    j = (k - 8) // 2
                    act.wait_ge(conv_done, 4 * p.j + j + 1)
                    if p.j:
                        act.wait_ge(back_t, 2 * p.j)
                    act.activation(silu_buf[:, j, :], conv_buf[:, j, :], ACT.Silu).then_inc(conv_silu, 1)
                pp = p.prev if not isinstance(p, Later) else None
                if pp is not None and pp.kind == "conv" and k == 2:
                    for t in range(NT):
                        act.wait_ge(back_t, 2 * pp.j + t + 1)
                        act.copy(qkv[:, pp.j // 2, t, BLK * (pp.j % 2):BLK * (pp.j % 2 + 1)],
                                 ps[:, 6 + t, :]).then_inc(back_copied, 1)
                if p.kind == "gate" and k == 3:
                    finished(p)
                    act.wait_ge(rstd_ready, p.norm + 1)
                    act.wait_ge(evac_dve, p.n_dve)
                    for t in range(NT):
                        act.activation(gs[:, t, :], acc(p, t), ACT.Silu,
                                       scale=rstd[:, p.norm, t:t + 1]).then_inc(evac_act, 1)
                if p.kind == "up" and k == 7:
                    for c in range(2):
                        act.wait_ge(turned, p.t0 + c + 1)
                        act.copy(fh[:, bass.ds(p.fkt + 2 * c, 2), :], halves(4 + c)).then_inc(turned_hi, 1)
                if p.kind == "resid":
                    if k == 4:
                        act.wait_ge(evac_dve, p.n_dve)
                        for t in range(NT):
                            square(p.norm + 1, p.j, t)
                    if k == 7:
                        for c in range(2):
                            split_x(COL[NORMS[p.norm + 1]], 4 * p.j + 2 * c, c, p.t0, p.h0)
                if p.kind == "v" and k == 3:
                    finished(p)
                    act.wait_ge(rstd_ready, p.norm + 1)
                    for t in range(NT):
                        act.activation(v_nat[:, t, BLK * p.j:BLK * (p.j + 1)], acc(p, t), ACT.Gelu,
                                       scale=rstd[:, p.norm, t:t + 1],
                                       accum_out=v_sum[:, t, p.j:p.j + 1]).then_inc(evac_act, 1)
                if p.kind == "v" and p.j == 3 and k in (5, 6):
                    t = k - 5
                    act.wait_ge(v_stat, 1)
                    act.activation(mixed[:, t, :], v_nat[:, t, :], ACT.Square, bias=v_nmu[:, t:t + 1],
                                   accum_out=v_var[:, t:t + 1]).then_inc(v_sq, 1)
                if p.kind == "u":
                    ka, _, _, kc = u_hooks(p)
                    if p.j == 0 and k in (5, 7, 9, 11):
                        pair = (k - 5) // 2
                        act.wait_ge(mix_mm, pair + 1)
                        for t in range(NT):
                            for gg in range(2):
                                g = 2 * pair + gg
                                act.activation(mixed[:, t, 256 * g:256 * (g + 1)], halves(6 + t)[:, gg, :],
                                               ACT.Identity, bias=cols[:, COL["b_s"] + g:COL["b_s"] + g + 1]
                                               ).then_inc(mix_out, 1)
                    if k == ka:
                        finished(p)
                        if p.j:
                            act.wait_ge(gated, 2 * p.j)
                        for t in range(NT):
                            act.activation(gs[:, t, :], acc(p, t), ACT.Gelu,
                                           scale=rstd[:, p.norm, t:t + 1]).then_inc(evac_act, 1)
                    if k == kc:
                        for c in range(2):
                            act.wait_ge(turned, p.t0 + c + 1)
                            act.copy(fh[:, 4 * p.j + 2 * c:4 * p.j + 2 * c + 2, :],
                                     halves(4 + c)).then_inc(turned_hi, 1)
                if p.kind in ("ga", "gc", "gp") and k == 3:
                    finished(p)
                    if p.kind == "gc":
                        act.wait_ge(f_mm, 5)
                    if p.kind == "gp":
                        act.wait_ge(gated, 10)
                    for t in range(NT):
                        dst = sga[:, t, BLK * p.j:BLK * (p.j + 1)] if p.kind == "ga" else gs[:, t, :]
                        act.activation(dst, acc(p, t), ACT.Silu,
                                       scale=rstd[:, 4, t:t + 1]).then_inc(evac_act, 1)
                if p.kind == "gc" and k == 8:
                    act.wait_ge(yc_ready, 2)
                    act.copy(fh[:, 8:12, :], ycT[:, :, :]).then_inc(yc_hi, 1)
                if p.kind == "fg" and k == 5:
                    act.wait_ge(f_in, 1)
                    link(act.activation(xn[:, :, :], xn[:, :, :], ACT.Exp))
                    act.activation(xn[:, :, :], xn[:, :, :], ACT.Ln, bias=1.0).then_inc(f_act, 1)
                if p.kind == "final" and k == 4:
                    act.wait_ge(evac_dve, p.n_dve)
                    for t in range(NT):
                        act.activation(gs[:, t, :], h[:, t, BLK * p.j:BLK * (p.j + 1)], ACT.Identity,
                                       accum_out=v_sum[:, t, p.j:p.j + 1]).then_inc(r_stat, 1)

            def during(blk, k):
                if blk.kind == "v" and blk.j == 0 and k == 3:
                    act.wait_ge(mm_done, blk.k0)
                    act.dma_start(ws_nat[:, :, :], a["odd_w_s"][0].rearrange("g t s -> t g s")).then_inc(ln_loaded, 16)
                    act.dma_start(ln_g_row[:, :], a["odd_ln_g"].to_broadcast([P, D])).then_inc(ln_loaded, 16)
                    act.dma_start(ln_b_row[:, :], a["odd_ln_b"].to_broadcast([P, D])).then_inc(ln_loaded, 16)
                if blk.b in heads_in:
                    n = heads_in[blk.b]
                    if k == 6:
                        act.wait_ge(h_nm, n + 1)
                        for t in range(NT):
                            act.activation(head_rows(t), head_rows(t), ACT.Exp, bias=f_nm[:, t:t + 1],
                                           accum_out=f_sm[:, t:t + 1]).then_inc(h_exp, 1)
                    if k == 9:
                        act.wait_ge(h_pt, n + 1)
                        act.copy(hd_pT[:, :, :], ps[:, 7, 0:3 * P].rearrange("p (c q) -> p c q", c=3)).then_inc(h_ptc, 1)
                    if k == 14:
                        act.wait_ge(h_yt, n + 1)
                        act.copy(fh[:, n, :], ps[:, 7, 0:SEQ]).then_inc(h_hi, 1)
                if blk.kind == "final" and blk.j == 0:
                    if k == 0:
                        act.wait_ge(mm_done, blk.k0)
                        act.dma_start(poolm[:, :, :, :], a["pool_consts"].rearrange("(t p) w q -> p t w q", p=P)
                                      ).then_inc(pool_loaded, 16)
                        act.dma_start(poolw[:, :, :], a["pool_w_2"][0].rearrange("g c d -> c g d")).then_inc(pool_loaded, 16)
                        act.dma_start(gf_row[:, :], a["final_norm"].unsqueeze(0).to_broadcast([P, D])).then_inc(gf_loaded, 16)
                        act.wait_ge(h_pv, 8)
                        act.dma_start(ln2_g_row[:, :], a["ln_g_2"].to_broadcast([P, D])).then_inc(ln2_loaded, 16)
                        act.dma_start(ln2_b_row[:, :], a["ln_b_2"].to_broadcast([P, D])).then_inc(ln2_loaded, 16)
                    if k == 11:
                        act.wait_ge(yp_ready, 4)
                        act.copy(fh[:, 12:16, :], pooled).then_inc(yp_hi, 1)

            def stream(blk, p, mixer, start):
                for k, slot, kk, loads in k_slots(blk):
                    if kk == 0:
                        act.wait_ge(raw_ready[slot], 16 * loads)
                    if blk.b or k >= RING:
                        act.wait_ge(mm_done, blk.k0 + k - RING + 1)
                    act.copy(w_hi[:, (blk.ring + k) % RING, 0:blk.width], raw[:, slot, kk, 0:blk.width]).then_inc(hi_ready, 1)
                    if p is not None:
                        after(p, k, blk)
                    during(blk, k)
                    if k >= start:
                        next(mixer, None)

            def delta():
                yield
                act.wait_ge(g_in, 1)
                link(act.activation(xn[:, :, :], xn[:, :, :], ACT.Exp))
                act.activation(xn[:, :, :], xn[:, :, :], ACT.Ln, bias=1.0)
                act.activation(a_exp, a_log, ACT.Exp)
                act.activation(beta[:, :, :], beta[:, :, :], ACT.Exp, scale=-1.0).then_inc(g_act, 1)
                for n, (src, t) in enumerate((s, t) for s in (qn, kn) for t in range(NT)):
                    if n >= 2:
                        act.wait_ge(l2_ms, n - 1)
                    act.activation((dD, dE)[n % 2][:, :, :], src[:, t, :].rearrange("p (h c) -> p h c", h=8),
                                   ACT.Square).then_inc(l2_sq, 1)
                    yield
                yield
                for m in range(8):
                    act.wait_ge(d_turned, m + 1)
                    dst = (dqT if m < 4 else dkT)[:, 2 * (m % 4):2 * (m % 4) + 2, :]
                    act.copy(dst, halves(4 + m % 4)).then_inc(d_copied, 1)
                    if m % 2:
                        yield
                for t in range(NT):
                    act.wait_ge(gam_ready, t + 1)
                    act.activation(e_gam[:, t, :], gam[:, t, :], ACT.Exp)
                    if t == 0:
                        act.activation(k_scale[:, 0, :], k_scale[:, 0, :], ACT.Exp)
                    else:
                        act.activation(q_dec[:, :, :], quarters(4, 2), ACT.Exp).then_inc(q_scale, 1)
                    yield
                    act.wait_ge(dec_in, t + 1)
                    act.activation(dL[:, :, :], dY[:, :, :], ACT.Exp, scale=-1.0).then_inc(dec_exp, 1)
                    yield
                    act.activation(dQK[:, :, :], dC[:, :, :], ACT.Exp).then_inc(dec_exp, 1)
                    yield
                    yield
                    yield
                    for lv in range(1, LEVELS):
                        for half in range(2):
                            n = (t * (LEVELS - 1) + lv - 1) * 2 + half
                            act.wait_ge(y_mm, n + 1)
                            act.copy(dY[:, 4 * half:4 * half + 4, :], quarters(y_bank(lv) + half)).then_inc(y_copied, 1)
                        yield
                        yield
                    if t == 1:
                        act.wait_ge(w_mm, 1)
                        act.mul(dY[:, :, :], quarters(6, 2), -1.0).then_inc(w_copied, 1)
                        yield
                        yield
                    else:
                        yield
                        act.wait_ge(s_mm, 1)
                        act.copy(S1[:, :, :], quarters(6, 2)).then_inc(s_ready, 1)
                        yield
                    act.wait_ge(o_mm, t + 1)
                    act.activation(dD[:, :, :], quarters(4, 2), ACT.Square).then_inc(o_sq, 1)
                    yield
                for _ in range(4):
                    yield
                turned_high(8, 0)

            def turned_high(kt, first):
                for m in range(4):
                    act.wait_ge(turned, even_resid[0].mix_t0 + first + m + 1)
                    act.copy(fh[:, kt + 2 * m:kt + 2 * m + 2, :], halves(4 + m % 2)).then_inc(turned_hi, 1)

            def attention():
                for m in range(9):
                    act.wait_ge(a_turned, m + 1)
                    dst = kTa[0:64, :, :] if m == 0 else qaT[0:64, 2 * m - 2:2 * m, :]
                    act.copy(dst, halves(4 + m % 4)[0:64]).then_inc(a_copied, 1)
                    if m % 2:
                        yield
                for s in range(len(UNITS) + 2):
                    if 1 <= s <= len(UNITS):
                        act.wait_ge(p_turned, s)
                        act.copy(e_pT[:, (s - 1) % 2], quarters(6)).then_inc(p_copied, 1)
                    if s < len(UNITS):
                        t, _, n = UNITS[s]
                        w = BLK // n
                        act.wait_ge(a_nm, s + 1)
                        for i in range(n):
                            act.activation(e_s[:, s % 2, w * i:w * (i + 1)], e_s[:, s % 2, w * i:w * (i + 1)],
                                           ACT.Exp, bias=e_nm[:, s % 2, i:i + 1],
                                           accum_out=e_sm[:, s % 3, i:i + 1])
                        act.activation(e_es[:, s % 3, 0:n], e_es[:, s % 3, 0:n], ACT.Exp).then_inc(a_exp_done, 1)
                    yield
                    yield
                turned_high(0, 4)

            run_blocks(act, stream, delta, attention, 4)
            after(blocks[-1], 4, None)
            act.wait_ge(r_stat, 8 + 1)
            for t in range(NT):
                if t:
                    act.wait_ge(r_sq, t)
                act.activation(junk[:, :], h[:, t, :], ACT.Square, bias=v_nmu[:, t:t + 1],
                               accum_out=v_var[:, t:t + 1]).then_inc(r_sq, 1)
            out_rows = out.rearrange("b (t p) d -> p (b t) d", p=P)
            for n in range(4):
                t, c = n // 2, n % 2
                act.wait_ge(fin_ready, n + 1)
                act.dma_start(out_rows[:, t, 1024 * c:1024 * (c + 1)], fin[:, t, 1024 * c:1024 * (c + 1)]).then_inc(stored, 16)
            act.wait_ge(stored, 64)

        @block.tensor
        def _(pe):
            def turn(rows, t0):
                for c in range(2):
                    if not isinstance(t0, int) or t0 + c >= 2:
                        pe.wait_ge(pt_read, t0 + c - 1)
                    for kk in range(2):
                        for t in range(NT):
                            ins = pe.transpose(halves(4 + c)[:, kk, P * t:P * (t + 1)], rows(t, 2 * c + kk), ident)
                    ins.then_inc(turned, 1)

            def rows_of(buf, at=0):
                return lambda t, j: buf[:, t, at + P * j:at + P * (j + 1)]

            pe.wait_ge(const_loaded, 16)
            pe.wait_ge(rows_loaded, 16 * (len(ROWS_A) + 1))
            pe.transpose(ps[:, 6, 0:N_ROWS_A], hb[0:N_ROWS_A, 0, 0:P], ident[0:N_ROWS_A, 0:N_ROWS_A])
            pe.transpose(ps[:, 6, N_ROWS_A:N_COLS], hb[0:N_ROWS_B, 1, 0:P],
                         ident[0:N_ROWS_B, 0:N_ROWS_B]).then_inc(cols_t, 1)
            pe.wait_ge(x_loaded, 16 * NT)
            for j in range(4):
                turn(rows_of(h, BLK * j), 2 * j)

            def wait_stationary(blk, k):
                if blk.kind == "final":
                    if k < 8:
                        pe.wait_ge(h_lo, k + 1)
                    elif k in (8, 12):
                        pe.wait_ge(yc_lo if k == 8 else yp_lo, 1)
                    return
                t0 = {"conv": lambda: 0, "gate": lambda: blk.prev.t0 - 6, "v": lambda: blk.prev.t0 - 6,
                      "fg": lambda: blk.prev.t0 - 6,
                      "half": lambda: blk.mix_t0,
                      "resid": lambda: (blk.mix_t0 + 4 if blk is even_resid[0] else
                                        by["u"][0].t0 if blk is odd_resid[0] else
                                        pairs[0 if blk is ffn_resid[0][0] else 1][0][1].t0)}[blk.kind]()
                if k % 2 == 0:
                    pe.wait_ge(pt_read, t0 + k // 2 + 1)

            def after(p, k, blk):
                if p.kind == "conv" and k == 3:
                    pe.wait_ge(evac_dve, p.n_dve)
                    turn(rows_of(hb), p.t0)
                if p.kind == "conv" and k == 14:
                    pe.wait_ge(conv_silu, 4 * (p.j + 1))
                    if p.j:
                        pe.wait_ge(back_copied, 2 * p.j)
                    for t in range(NT):
                        for c in range(4):
                            ins = pe.transpose(ps[:, 6 + t, P * c:P * (c + 1)], silu_buf[:, c, P * t:P * (t + 1)], ident)
                        ins.then_inc(back_t, 1)
                if p.kind == "resid" and k == 3:
                    pe.wait_ge(evac_dve, p.n_dve)
                    turn(rows_of(h, BLK * p.j), p.t0)
                if p.kind in ("up", "ch", "k2", "q2") and k == 3:
                    pe.wait_ge(evac_dve, p.n_dve)
                    turn(rows_of(hb), p.t0)
                if p.kind == "u":
                    if p.j == 0 and k in (1, 3, 5, 7):
                        pair = (k - 1) // 2
                        if pair == 0:
                            pe.wait_ge(ws_ready, 1)
                            pe.wait_ge(v_done, 4)
                        else:
                            pe.wait_ge(mix_out, 4 * pair)
                        for t in range(NT):
                            for gg in range(2):
                                g = 2 * pair + gg
                                ins = pe.matmul(halves(6 + t)[:, gg, :], wsT[:, g, :],
                                                v_nat[:, t, 256 * g:256 * (g + 1)], start=True, stop=True)
                        ins.then_inc(mix_mm, 1)
                    if k == u_hooks(p)[2]:
                        pe.wait_ge(gated, 2 * (p.j + 1))
                        turn(rows_of(hb), p.t0)
                if p.kind == "gc" and k == 4:
                    pe.wait_ge(gated, 10)
                    turn(rows_of(hb), p.t0)
                if p.kind == "gp" and k == 4:
                    pe.wait_ge(evac_act, p.n_act)
                    turn(rows_of(gs), p.t0)
                if p.kind == "fg" and k == 8:
                    pe.wait_ge(f_lf, 1)
                    pe.matmul(ps[:, 7, 0:8], upper, xa[:, 0, :], start=True, stop=True)
                    pe.matmul(ps[:, 7, 8:16], ones, xa[:, 0, :], start=True, stop=False)
                    pe.matmul(ps[:, 7, 8:16], upper, xa[:, 1, :], start=False, stop=True).then_inc(f_mm, 1)
                if p.kind == "k2" and p.j == 0 and k in (1, 4, 7, 10):
                    m = (k - 1) // 3
                    pe.wait_ge(f_lf, 3)
                    pe.wait_ge(f_copied, m)
                    for i in range(2):
                        dst = halves(6 + m % 2)[:, i, :]
                        pe.matmul(dst, lf_rows(0)[:, 2 * m + i, :], upper_ones, start=True, stop=False)
                        ins = pe.matmul(dst[:, P:2 * P], lf_rows(1)[:, 2 * m + i, :], upper, start=False, stop=True)
                    ins.then_inc(f_mm, 1)

            def during(blk, k):
                if blk.kind == "v" and blk.j == 1 and k == 3:
                    pe.wait_ge(ln_loaded, 48)
                    for g in range(8):
                        ins = pe.transpose(quarters(6, 2)[:, g, :], ws_nat[:, g, :], ident)
                    ins.then_inc(ws_turned, 1)
                if blk.b in heads_in:
                    n = heads_in[blk.b]
                    if k == 1:
                        pe.wait_ge(pt_read, by["q2"][n // 4].t0 + 2)
                        pe.wait_ge(f_copied, 5)
                        if n:
                            pe.wait_ge(h_ya, 2 * n)
                        pe.matmul(ps[:, 6, 0:P], qT2[:, n, 0:P], kT2[:, n, 0:P], start=True, stop=True)
                        pe.matmul(ps[:, 6, P:3 * P], qT2[:, n, P:2 * P], kT2[:, n, :],
                                  start=True, stop=True).then_inc(h_scored, 1)
                    if k == 5:
                        pe.wait_ge(h_exp, 2 * (n + 1))
                        if n:
                            pe.wait_ge(h_lo, n)
                        for c in range(3):
                            ins = pe.transpose(ps[:, 7, P * c:P * (c + 1)], hd_s[:, P * c:P * (c + 1)], ident)
                        ins.then_inc(h_pt, 1)
                    if k == 8:
                        pe.wait_ge(h_ptc, n + 1)
                        pe.wait_ge(evac_dve, by["v2"][n // 4].n_dve)
                        vh = slice(P * n, P * (n + 1))
                        pe.matmul(ps[:, 6, 0:P], hd_pT[:, 0, :], v2[:, 0, vh], start=True, stop=True)
                        pe.matmul(ps[:, 6, P:2 * P], hd_pT[:, 1, :], v2[:, 0, vh], start=True, stop=False)
                        pe.matmul(ps[:, 6, P:2 * P], hd_pT[:, 2, :], v2[:, 1, vh],
                                  start=False, stop=True).then_inc(h_pv, 1)
                    if k == 11:
                        pe.wait_ge(h_ya, 2 * (n + 1))
                        for t in range(NT):
                            ins = pe.transpose(ps[:, 7, P * t:P * (t + 1)], ya[:, t, :], ident)
                        ins.then_inc(h_yt, 1)
                if blk.kind == "final" and blk.j == 0:
                    if k == 2:
                        pe.wait_ge(pool_loaded, 32)
                        pe.wait_ge(evac_dve, by["pu"][0].n_dve)
                        for g in range(4):
                            for t in range(NT):
                                ins = pe.matmul(halves(6 + g // 2)[:, g % 2, :], pun[:, t, P * g:P * (g + 1)],
                                                poolm[:, t, g, :], start=(t == 0), stop=(t == 1))
                        ins.then_inc(z_mm, 1)
                    if k == 5:
                        pe.wait_ge(z_copied, 2)
                        for g in range(4):
                            ins = pe.matmul(halves(6 + g // 2)[:, g % 2, :], poolw[:, g, :], zT[:, g, :],
                                            start=True, stop=True)
                        ins.then_inc(pw_mm, 1)

            def stream(blk, p, mixer, start):
                if isinstance(blk, Later):
                    pe.wait_ge(*((evac_act, blk.n_act - 2) if blk.by_act else (evac_dve, blk.n_dve - 2)))
                elif blk.b >= 2:
                    old = blocks[blk.b - 2]
                    pe.wait_ge(*((evac_act, old.n_act) if old.by_act else (evac_dve, old.n_dve)))
                hi_x, lo_x = (xh, xl) if blk.lhs == "x" else (fh, fl)
                for k, _, _, _ in k_slots(blk):
                    if blk.first:
                        wait_stationary(blk, k)
                    pe.wait_ge(lo_ready, blk.k0 + k + 1)
                    hi_w, lo_w = w_hi[:, (blk.ring + k) % RING, 0:blk.width], w_lo[:, (blk.ring + k) % RING, 0:blk.width]
                    for t in range(NT):
                        tok = slice(P * t, P * (t + 1))
                        pe.matmul(acc(blk, t), hi_x[:, blk.kt0 + k, tok], hi_w, start=(k == 0), stop=False)
                        pe.matmul(acc(blk, t), hi_x[:, blk.kt0 + k, tok], lo_w, start=False, stop=False)
                        ins = pe.matmul(acc(blk, t), lo_x[:, blk.kt0 + k, tok], hi_w, start=False, stop=(k == blk.nk - 1))
                    ins.then_inc(mm_done, 1)
                    if p is not None:
                        after(p, k, blk)
                    during(blk, k)
                    if k >= start:
                        next(mixer, None)

            def delta():
                for _ in range(6):
                    yield
                pe.wait_ge(pt_read, by["conv"][5].t0 + 2)
                pe.wait_ge(back_copied, 12)
                for m in range(8):
                    src = qn if m < 4 else kn
                    pe.wait_ge(l2_q if m < 4 else l2_k, 2)
                    if m >= 4:
                        pe.wait_ge(d_copied, m - 3)
                    for i in range(2):
                        for t in range(NT):
                            hd = 2 * (m % 4) + i
                            ins = pe.transpose(halves(4 + m % 4)[:, i, P * t:P * (t + 1)],
                                               src[:, t, P * hd:P * (hd + 1)], ident)
                    ins.then_inc(d_turned, 1)
                    if m % 2:
                        yield
                for t in range(NT):
                    tok = slice(P * t, P * (t + 1))
                    pe.wait_ge(ug_ready, t + 1)
                    if t == 0:
                        pe.wait_ge(d_copied, 8)
                    else:
                        pe.wait_ge(o_done, 1)
                        pe.wait_ge(s_ready, 1)
                    for half in range(2):
                        pe.matmul(ps[:, 4 + half, :], ones, dC[:, 4 * half:4 * half + 4, :], start=True, stop=True)
                    pe.matmul(ps[:, 6, 0:8], upper, g_log[:, t, :], start=True, stop=True).then_inc(gam_mm, 1)
                    yield
                    pe.wait_ge(gam_ready, t + 1)
                    for hd in range(8):
                        ins = pe.matmul(quarters(6, 2)[:, hd, :], dkT[:, hd, tok], dkT[:, hd, tok], start=True, stop=True)
                    ins.then_inc(kq_mm, 1)
                    yield
                    pe.wait_ge(dec_in, t + 1)
                    for hd in range(8):
                        ins = pe.matmul(quarters(4, 2)[:, hd, :], dkT[:, hd, tok], dqT[:, hd, tok], start=True, stop=True)
                    ins.then_inc(kq_mm, 1)
                    yield
                    yield
                    for half in range(2):
                        pe.wait_ge(c_ready, LEVELS * t + 1)
                        for i in range(4):
                            ins = pe.matmul(quarters(6 + half)[:, i, :], dC[:, 4 * half + i, :], ident, start=True, stop=True)
                        ins.then_inc(de_mm, 1)
                    yield
                    for lv in range(1, LEVELS):
                        for half in range(2):
                            pe.wait_ge(c_ready, LEVELS * t + lv + 1)
                            pe.wait_ge(de_ready, 2 * (LEVELS * t + lv - 1) + half + 1)
                            if lv == 1 and half == 0:
                                pe.wait_ge(lqk_ready, 2 * t + 2)
                            if half == 1:
                                pe.wait_ge(de_ready, 2 * (LEVELS * t + lv))
                            for i in range(4):
                                hd = 4 * half + i
                                ins = pe.matmul(quarters(y_bank(lv) + half)[:, i, :], dC[:, hd, :], dE[:, hd, :], start=True, stop=True)
                            ins.then_inc(y_mm, 1)
                        yield
                        for half in range(2):
                            pe.wait_ge(y_copied, 2 * ((LEVELS - 1) * t + lv - 1) + 1 + half)
                            for i in range(4):
                                hd = 4 * half + i
                                if lv < LEVELS - 1:
                                    pe.matmul(quarters(de_bank(lv, half))[:, i, :], dY[:, hd, :], dD[:, hd, :], start=True, stop=True)
                                ins = pe.matmul(quarters(de_bank(lv, half) + 1)[:, i, :], dD[:, hd, :], dY[:, hd, :],
                                                start=True, stop=True)
                            ins.then_inc(de_mm, 1)
                        yield
                    pe.wait_ge(de_ready, 2 * LEVELS * (t + 1))
                    pe.wait_ge(kv_ready, t + 1)
                    if t == 1:
                        for hd in range(8):
                            ins = pe.matmul(quarters(6, 2)[:, hd, :], dkb[:, hd, :], dE[:, hd, :], start=True, stop=True)
                        ins.then_inc(w_mm, 1)
                        yield
                        pe.wait_ge(w_copied, 1)
                    for hd in range(8):
                        ins = pe.matmul(quarters(4, 2)[:, hd, :], dE[:, hd, :], vn[:, t, P * hd:P * (hd + 1)],
                                        start=True, stop=(t == 0))
                        if t == 1:
                            ins = pe.matmul(quarters(4, 2)[:, hd, :], dY[:, hd, :], S1[:, hd, :], start=False, stop=True)
                    ins.then_inc(u_mm, 1)
                    yield
                    pe.wait_ge(vnew_ready, t + 1)
                    if t == 0:
                        for hd in range(8):
                            ins = pe.matmul(quarters(6, 2)[:, hd, :], dkb[:, hd, :], v_new[:, hd, :], start=True, stop=True)
                        ins.then_inc(s_mm, 1)
                        yield
                    for hd in range(8):
                        if t == 1:
                            pe.matmul(quarters(4, 2)[:, hd, :], q_dec[:, hd, :], S1[:, hd, :], start=True, stop=False)
                        ins = pe.matmul(quarters(4, 2)[:, hd, :], dQK[:, hd, :], v_new[:, hd, :], start=(t == 0), stop=True)
                    ins.then_inc(o_mm, 1)
                    yield
                for _ in range(4):
                    yield
                pe.wait_ge(o_done, 2)
                for j in range(2):
                    turn(rows_of(qn, BLK * j), even_resid[0].mix_t0 + 2 * j)

            def attention():
                pe.wait_ge(evac_dve, by["qa"][1].n_dve)
                pe.wait_ge(pt_read, even_resid[0].mix_t0 + 4)
                for m in range(9):
                    if m >= 4:
                        pe.wait_ge(a_copied, m - 3)
                    for i in range(2):
                        for t in range(NT):
                            at = A_Q + 64 * i if m == 0 else 64 * (2 * m - 2 + i)
                            ins = pe.transpose(halves(4 + m % 4)[0:64, i, P * t:P * (t + 1)], att[:, t, at:at + 64], ident)
                    ins.then_inc(a_turned, 1)
                    if m % 2:
                        yield
                pe.wait_ge(a_copied, 9)
                for s in range(len(UNITS) + 2):
                    if s >= 2:
                        t, h0, n = UNITS[s - 2]
                        pe.wait_ge(p_copied, s - 1)
                        if s >= 3:
                            pe.wait_ge(a_out, s - 2)
                        for i in range(n):
                            for kb in range(t + 1):
                                g = (h0 + i) // 8
                                ins = pe.matmul(ps[:, 7, 64 * i:64 * i + 64], e_pT[:, s % 2, (t + 1) * i + kb, :],
                                                att[:, kb, 1152 + 64 * g:1216 + 64 * g], start=(kb == 0), stop=(kb == t))
                        ins.then_inc(pv_done, 1)
                    if 1 <= s <= len(UNITS):
                        pe.wait_ge(a_exp_done, s)
                        if s >= 2:
                            pe.wait_ge(p_copied, s - 1)
                        for c in range(4):
                            ins = pe.transpose(quarters(6)[:, c, :], e_s[:, (s - 1) % 2, P * c:P * (c + 1)], ident)
                        ins.then_inc(p_turned, 1)
                    if s < len(UNITS):
                        t, h0, n = UNITS[s]
                        w = BLK // n
                        if s >= 2:
                            pe.wait_ge(a_nm, s - 1)
                        for i in range(n):
                            ins = pe.matmul(ps[:, 4 + s % 2, w * i:w * (i + 1)], qaT[0:64, h0 + i, P * t:P * (t + 1)],
                                            kTa[0:64, (h0 + i) // 8, 0:w], start=True, stop=True)
                        ins.then_inc(scored, 1)
                    yield
                    yield
                pe.wait_ge(a_out, len(UNITS))
                for j in range(2):
                    turn(rows_of(att, BLK * j), even_resid[0].mix_t0 + 4 + 2 * j)

            run_blocks(pe, stream, delta, attention)

        @block.vector
        def _(dve):
            link = linker(dve, dve_link)
            STT, TT, TS = dve.scalar_tensor_tensor, dve.tensor_tensor, dve.tensor_scalar

            def spread(v, n, last=P):
                return v.unsqueeze(2).to_broadcast([P, n, last])

            def each(v, n):
                return v.unsqueeze(1).to_broadcast([P, n, v.shape[1]])

            def heads(v):
                return v.rearrange("p (h c) -> p h c", h=8)

            dve.wait_ge(cols_t, 1)
            dve.tensor_copy(cols[:, :], ps[:, 6, 0:N_COLS]).then_inc(cols_ready, 1)
            dve.wait_ge(cols_ready, 1)

            def low_x(gain, kt, c, h0):
                dve.wait_ge(turned_hi, h0 + c + 1)
                for kk in range(2):
                    ins = STT(xl[:, kt + kk, :], halves(4 + c)[:, kk, :], cols[:, gain + kt + kk:gain + kt + kk + 1],
                              xh[:, kt + kk, :].bitcast(F32), ALU.mult, ALU.subtract)
                ins.then_inc(pt_read, 1)

            for m in range(T_INIT):
                low_x(COL["even_norm"], 2 * m, m % 2, m - m % 2)

            def mean_square(n):
                dve.wait_ge(sq_done, 8 * (n + 1))
                if n:
                    dve.wait_ge(rstd_ready, n)
                link(dve.tensor_reduce(ms, ssq[:, n], AX.X, ALU.add))
                TS(ms, ms, 1.0 / D, EPS, ALU.mult, ALU.add).then_inc(ms_ready, 1)

            mean_square(0)

            def finished(p):
                dve.wait_ge(mm_done, p.k0 + p.nk)
                dve.wait_ge(rstd_ready, p.norm + 1)

            counts = {}

            def conv(j, taps, col, stride, src, dst, done, last_of_bank):
                for i in reversed(range(taps)):
                    lag = taps - 1 - i
                    w = cols[:, col + stride * i + j:col + stride * i + j + 1]
                    if lag == 0:
                        ins = TS(dst, src, w, None, ALU.mult)
                    else:
                        ins = STT(dst[:, lag:SEQ], src[:, 0:SEQ - lag], w, dst[:, lag:SEQ], ALU.mult, ALU.add)
                    if i:
                        link(ins)
                ins.then_inc(done, 1)
                if last_of_bank:
                    counts[done.name] = counts.get(done.name, 0) + 2
                    dve.wait_ge(done, counts[done.name])
                    dve.sem_inc(pt_read, 1)

            def after(p, k, blk):
                if p.kind == "kvba" and k == 3:
                    finished(p)
                    for t in range(NT):
                        r = rstd[:, 0, t:t + 1]
                        TS(att[:, t, A_Q:A_Q + 256], acc(p, t)[:, 0:256], r, None, ALU.mult)
                        TS(beta[:, t, :], acc(p, t)[:, 256:264], r, None, ALU.mult)
                        TS(xa[:, t, :], acc(p, t)[:, 264:272], r, None, ALU.mult).then_inc(evac_dve, 1)
                if p.kind == "qa" and k == 3:
                    finished(p)
                    for t in range(NT):
                        TS(att[:, t, BLK * p.j:BLK * (p.j + 1)], acc(p, t), rstd[:, 0, t:t + 1], None,
                           ALU.mult).then_inc(evac_dve, 1)
                if p.kind in ("conv", "k2", "q2") and k == 3:
                    finished(p)
                    dve.wait_ge(turned, p.t0)
                    for t in range(NT):
                        TS(hb[:, t, :], acc(p, t), rstd[:, p.norm, t:t + 1], None, ALU.mult).then_inc(evac_dve, 1)
                if p.kind == "conv" and k in (7, 9, 11, 13):
                    j = (k - 7) // 2
                    dve.wait_ge(turned, p.t0 + j // 2 + 1)
                    if p.j:
                        dve.wait_ge(conv_silu, 4 * (p.j - 1) + j + 1)
                    conv(4 * p.j + j, 4, COL["conv"], 24, halves(4 + j // 2)[:, j % 2, :], conv_buf[:, j, :],
                         conv_done, j % 2 == 1)
                if p.kind in ("half", "resid"):
                    if k == 3:
                        dve.wait_ge(mm_done, p.k0 + p.nk)
                        for t in range(NT):
                            hs = h[:, t, BLK * p.j:BLK * (p.j + 1)]
                            TT(hs, acc(p, t), hs, ALU.add).then_inc(evac_dve, 1)
                if p.kind == "resid":
                    if k == 7:
                        for c in range(2):
                            low_x(COL[NORMS[p.norm + 1]], 4 * p.j + 2 * c, c, p.h0)
                    if k == 9 and p.j == 3:
                        mean_square(p.norm + 1)
                if p.kind == "up" and k == 3:
                    finished(p)
                    dve.wait_ge(evac_act, p.n_act)
                    dve.wait_ge(turned, p.t0)
                    for t in range(NT):
                        STT(hb[:, t, :], acc(p, t), rstd[:, p.norm, t:t + 1], gs[:, t, :], ALU.mult,
                            ALU.mult).then_inc(evac_dve, 1)
                if p.kind == "up" and k == 7:
                    low_f(p)
                if p.kind == "v" and p.j == 3 and k == 4:
                    dve.wait_ge(evac_act, p.n_act)
                    link(dve.tensor_reduce(v_mu, v_sum[:, :, :], AX.X, ALU.add))
                    link(TS(v_mu, v_mu, 1.0 / D, None, ALU.mult))
                    TS(v_nmu, v_mu, -1.0, None, ALU.mult).then_inc(v_stat, 1)
                if p.kind == "v" and p.j == 3 and k in (7, 8, 9, 10, 11, 12, 13, 14):
                    n = (k - 7) % 4
                    t, part = n // 2, slice(1024 * (n % 2), 1024 * (n % 2 + 1))
                    if k < 11:
                        dve.wait_ge(v_sq, t + 1)
                        dve.wait_ge(ln_loaded, 48)
                        STT(v_nat[:, t, part], v_nat[:, t, part], v_mu[:, t:t + 1], ln_g_row[:, part], ALU.subtract,
                            ALU.mult).then_inc(v_done, 1)
                    else:
                        dve.wait_ge(v_rs, 1)
                        dve.wait_ge(v_done, 4)
                        STT(v_nat[:, t, part], v_nat[:, t, part], v_rstd[:, t:t + 1], ln_b_row[:, part], ALU.mult,
                            ALU.add).then_inc(v_done, 1)
                    if k == 8:
                        dve.wait_ge(v_sq, 2)
                        TS(v_var, v_var, 1.0 / D, EPS, ALU.mult, ALU.add).then_inc(v_ms, 1)
                if p.kind == "u":
                    _, kb, _, kc = u_hooks(p)
                    if k == kb:
                        dve.wait_ge(evac_act, p.n_act)
                        dve.wait_ge(mix_out, 16 if p.j else 4)
                        dve.wait_ge(turned, p.t0)
                        for t in range(NT):
                            TT(hb[:, t, :], gs[:, t, :], mixed[:, t, BLK * p.j:BLK * (p.j + 1)],
                               ALU.mult).then_inc(gated, 1)
                    if k == kc:
                        low_f(p)
                if p.kind == "fg":
                    if k == 3:
                        finished(p)
                        for t in range(NT):
                            TS(xa[:, t, :], acc(p, t), rstd[:, 4, t:t + 1], None, ALU.mult).then_inc(evac_dve, 1)
                    if k == 4:
                        dve.wait_ge(evac_dve, p.n_dve)
                        link(TT(xa[:, :, :], xa[:, :, :], each(b_f, NT), ALU.add))
                        minus_abs().then_inc(f_in, 1)
                    if k == 6:
                        dve.wait_ge(f_act, 1)
                        STT(xa[:, :, :], xa[:, :, :], 0.0, xn[:, :, :], ALU.min, ALU.subtract).then_inc(f_lf, 1)
                        dve.wait_ge(f_lf, 1)
                        for t in range(NT):
                            TT(lf_rows(t), each(ones, 8), spread(xa[:, t, :], 8), ALU.mult).then_inc(f_lf, 1)
                    if k == 12:
                        dve.wait_ge(f_mm, 1)
                        dve.tensor_copy(gam[:, :, :], ps[:, 7, 0:16].rearrange("p (t c) -> p t c", t=NT)
                                        ).then_inc(f_copied, 1)
                if p.kind == "k2" and p.j == 0 and k in (5, 8, 11, 14):
                    m = (k - 5) // 3
                    dve.wait_ge(f_mm, m + 2)
                    dve.tensor_copy(cum_row[:, 2 * m:2 * m + 2, :], halves(6 + m % 2)).then_inc(f_copied, 1)
                if p.kind in ("k2", "q2") and k == 7:
                    for c in range(2):
                        dve.wait_ge(turned, p.t0 + c + 1)
                        dst = (kT2 if p.kind == "k2" else qT2)[:, 4 * p.j + 2 * c:4 * p.j + 2 * c + 2, :]
                        dve.tensor_copy(dst, halves(4 + c)).then_inc(pt_read, 1)
                if p.kind in ("v2", "cc", "cb", "pu") and k == 3:
                    finished(p)
                    if p.kind == "cc":
                        dve.wait_ge(f_mm, 5)
                    for t in range(NT):
                        dst = {"v2": lambda: v2[:, t, BLK * p.j:BLK * (p.j + 1)], "cc": lambda: ccn[:, t, :],
                               "cb": lambda: ccn[:, t, :], "pu": lambda: pun[:, t, :]}[p.kind]()
                        TS(dst, acc(p, t), rstd[:, 4, t:t + 1], None, ALU.mult).then_inc(evac_dve, 1)
                if p.kind == "ch":
                    if k == 3:
                        finished(p)
                        dve.wait_ge(turned, p.t0)
                        dve.wait_ge(evac_dve, p.prev.n_dve)
                        for t in range(NT):
                            STT(hb[:, t, :], acc(p, t), rstd[:, 4, t:t + 1], ccn[:, t, :], ALU.mult,
                                ALU.mult).then_inc(evac_dve, 1)
                    if k in (7, 9, 11, 13):
                        j = (k - 7) // 2
                        dve.wait_ge(turned, p.t0 + j // 2 + 1)
                        conv(j, 3, COL["conv2"], 4, halves(4 + j // 2)[:, j % 2, :], ycT[:, j, :], yc_conv, j % 2 == 1)
                if p.kind == "gc":
                    if k == 4:
                        dve.wait_ge(evac_act, p.n_act)
                        dve.wait_ge(evac_dve, by["cb"][0].n_dve)
                        dve.wait_ge(turned, p.t0)
                        for t in range(NT):
                            TT(hb[:, t, :], gs[:, t, :], ccn[:, t, :], ALU.mult).then_inc(gated, 1)
                    if k == 7:
                        dve.wait_ge(yc_conv, 4)
                        for c in range(2):
                            dve.wait_ge(turned, p.t0 + c + 1)
                            link(TT(ycT[:, 2 * c:2 * c + 2, :], halves(4 + c), ycT[:, 2 * c:2 * c + 2, :], ALU.mult))
                            dve.sem_inc(pt_read, 1)
                            dve.sem_inc(yc_ready, 1)
                    if k == 9:
                        dve.wait_ge(yc_hi, 1)
                        TT(fl[:, 8:12, :], ycT[:, :, :], fh[:, 8:12, :].bitcast(F32), ALU.subtract).then_inc(yc_lo, 1)
                if p.kind == "gp" and k == 7:
                    for c in range(2):
                        dve.wait_ge(turned, p.t0 + c + 1)
                        dve.tensor_copy(spT[:, 2 * c:2 * c + 2, :], halves(4 + c)).then_inc(pt_read, 1)
                if p.kind == "final" and k == 3:
                    dve.wait_ge(mm_done, p.k0 + p.nk)
                    dve.wait_ge(x_out, 4)
                    for t in range(NT):
                        hs = h[:, t, BLK * p.j:BLK * (p.j + 1)]
                        STT(hs, hs, ALPHA, acc(p, t), ALU.mult, ALU.add).then_inc(evac_dve, 1)

            def low_f(p):
                for c in range(2):
                    dve.wait_ge(turned_hi, p.h0 + c + 1)
                    kt = bass.ds(p.fkt + 2 * c, 2)
                    TT(fl[:, kt, :], halves(4 + c), fh[:, kt, :].bitcast(F32), ALU.subtract).then_inc(pt_read, 1)

            def minus_abs():
                link(TS(xn[:, :, :], xa[:, :, :], -1.0, None, ALU.mult))
                ins = TT(xn[:, :, :], xn[:, :, :], xa[:, :, :], ALU.min)
                return ins

            def during(blk, k):
                if blk.kind == "v" and blk.j == 1 and k == 6:
                    dve.wait_ge(ws_turned, 1)
                    TT(wsT[:, :, :], quarters(6, 2), each(upper, 8), ALU.mult).then_inc(ws_ready, 1)
                if blk.b in heads_in:
                    n = heads_in[blk.b]
                    if k == 5:
                        dve.wait_ge(f_copied, 5)
                        if n:
                            dve.wait_ge(h_pt, n)
                        link(STT(hd_s[:, 0:P], cum_row[:, n, 0:P], gam[:, 0, n:n + 1], m_causal, ALU.subtract, ALU.subtract))
                        link(TS(hd_s[:, P:2 * P], cum_row[:, n, 0:P], gam[:, 1, n:n + 1], None, ALU.subtract))
                        link(STT(hd_s[:, 2 * P:3 * P], cum_row[:, n, P:2 * P], gam[:, 1, n:n + 1], m_causal,
                                 ALU.subtract, ALU.subtract))
                        dve.wait_ge(h_scored, n + 1)
                        link(STT(hd_s[:, :], ps[:, 6, 0:3 * P], B_HD ** -0.5, hd_s[:, :], ALU.mult, ALU.subtract))
                        link(dve.tensor_reduce(f_nm[:, 0:1], head_rows(0), AX.X, ALU.max, negate=True))
                        dve.tensor_reduce(f_nm[:, 1:2], head_rows(1), AX.X, ALU.max, negate=True).then_inc(h_nm, 1)
                    if k == 12:
                        dve.wait_ge(h_exp, 2 * (n + 1))
                        link(dve.reciprocal(f_rd, f_sm))
                        dve.wait_ge(h_pv, n + 1)
                        dve.wait_ge(evac_act, by["ga"][n // 4].n_act)
                        if n:
                            dve.wait_ge(h_yt, n)
                        for t in range(NT):
                            STT(ya[:, t, :], ps[:, 6, P * t:P * (t + 1)], f_rd[:, t:t + 1],
                                sga[:, t, P * n:P * (n + 1)], ALU.mult, ALU.mult).then_inc(h_ya, 1)
                    if k == 15:
                        dve.wait_ge(h_hi, n + 1)
                        TT(fl[:, n, :], ps[:, 7, 0:SEQ], fh[:, n, :].bitcast(F32), ALU.subtract).then_inc(h_lo, 1)
                if blk.kind == "final" and blk.j == 0:
                    if k == 5:
                        dve.wait_ge(z_mm, 1)
                        for c in range(2):
                            dve.tensor_copy(zT[:, 2 * c:2 * c + 2, :], halves(6 + c)).then_inc(z_copied, 1)
                    if k == 8:
                        dve.wait_ge(pw_mm, 1)
                        dve.wait_ge(pt_read, by["gp"][0].t0 + 2)
                        dve.wait_ge(turned, by["gc"][0].t0 + 2)
                        for g in range(4):
                            c = COL["pool_scale"] + g
                            STT(pooled[:, g, :], halves(6 + g // 2)[:, g % 2, :], cols[:, c:c + 1], spT[:, g, :],
                                ALU.mult, ALU.mult).then_inc(yp_ready, 1)
                    if k == 11:
                        dve.wait_ge(yp_hi, 1)
                        TT(fl[:, 12:16, :], pooled, fh[:, 12:16, :].bitcast(F32), ALU.subtract).then_inc(yp_lo, 1)
                    if k in (12, 13, 14, 15):
                        dve.wait_ge(gf_loaded, 16)
                        t, c = (k - 12) // 2, slice(1024 * (k % 2), 1024 * (k % 2 + 1))
                        STT(h[:, t, c], h[:, t, c], rstd[:, 4, t:t + 1], gf_row[:, c], ALU.mult,
                            ALU.mult).then_inc(x_out, 1)

            def stream(blk, p, mixer, start):
                for k, slot, kk, _ in k_slots(blk):
                    dve.wait_ge(hi_ready, blk.k0 + k + 1)
                    w = blk.width
                    TT(w_lo[:, (blk.ring + k) % RING, 0:w], raw[:, slot, kk, 0:w], w_hi[:, (blk.ring + k) % RING, 0:w].bitcast(F32),
                       ALU.subtract).then_inc(lo_ready, 1)
                    if p is not None:
                        after(p, k, blk)
                    during(blk, k)
                    if k >= start:
                        next(mixer, None)

            def delta():
                dve.wait_ge(small_loaded, 80)
                link(TS(n_sinks, sinks, -1.0, None, ALU.mult))
                dve.wait_ge(evac_dve, by["kvba"][0].n_dve)
                link(TT(xa[:, :, :], xa[:, :, :], each(dt_bias, NT), ALU.add))
                minus_abs().then_inc(g_in, 1)
                yield
                dve.wait_ge(g_act, 1)
                link(STT(xa[:, :, :], xa[:, :, :], 0.0, xn[:, :, :], ALU.max, ALU.add))
                STT(g_log[:, :, :], xa[:, :, :], -1.0, each(a_exp, NT), ALU.mult, ALU.mult).then_inc(g_ready, 1)
                link(TS(beta[:, :, :], beta[:, :, :], 1.0, None, ALU.add))
                link(dve.reciprocal(beta[:, :, :], beta[:, :, :]))
                for n in range(4):
                    dve.wait_ge(l2_sq, n + 1)
                    dve.tensor_reduce(l2_ss[:, n // 2, n % 2, :], (dD, dE)[n % 2][:, :, :], AX.X,
                                      ALU.add).then_inc(l2_ms, 1)
                    yield
                dve.wait_ge(l2_ms, 4)
                TS(l2_ss[:, :, :, :], l2_ss[:, :, :, :], EPS, None, ALU.add).then_inc(l2_ms, 1)
                dve.wait_ge(l2_rs, 1)
                for t in range(NT):
                    TT(heads(kn[:, t, :]), heads(kn[:, t, :]), spread(l2_r[:, 1, t, :], 8), ALU.mult).then_inc(l2_k, 1)
                yield
                for _ in range(3):
                    yield
                for t in range(NT):
                    tok = slice(P * t, P * (t + 1))
                    if t:
                        dve.wait_ge(de_mm, 2 * LEVELS)
                    dve.wait_ge(g_ready, 1)
                    TT(dC[:, :, :], each(upper, 8), spread(g_log[:, t, :], 8), ALU.mult).then_inc(ug_ready, 1)
                    if t == 0:
                        yield
                    dve.wait_ge(gam_mm, t + 1)
                    link(dve.tensor_copy(gam[:, t, :], ps[:, 6, 0:8]))
                    if t == 0:
                        link(TT(k_scale[:, 0, :], quarters(4, 2)[:, :, P - 1], gam[:, 0, :], ALU.subtract))
                    dve.sem_inc(gam_ready, 1)
                    if t == 1:
                        dve.wait_ge(q_scale, 1)
                    link(TT(dY[:, :, :], quarters(4, 2), spread(gam[:, t, :], 8), ALU.subtract))
                    link(TS(dC[:, :, :], dY[:, :, :], 0.0, None, ALU.min))
                    TS(dY[:, :, :], dY[:, :, :], 0.0, None, ALU.max).then_inc(dec_in, 1)
                    yield
                    yield
                    dve.wait_ge(dec_exp, 2 * t + 1)
                    dve.wait_ge(kq_mm, 2 * t + 1)
                    link(TT(dL[:, :, :], quarters(6, 2), dL[:, :, :], ALU.mult))
                    TT(dL[:, :, :], dL[:, :, :], spread(beta[:, t, :], 8), ALU.mult).then_inc(lqk_ready, 1)
                    yield
                    dve.wait_ge(dec_exp, 2 * t + 2)
                    link(TT(dQK[:, :, :], dQK[:, :, :], each(upper, 8), ALU.mult))
                    dve.wait_ge(kq_mm, 2 * t + 2)
                    TT(dQK[:, :, :], quarters(4, 2), dQK[:, :, :], ALU.mult).then_inc(lqk_ready, 1)
                    dve.wait_ge(c_ready, LEVELS * t + 1)
                    for half in range(2):
                        four = slice(4 * half, 4 * half + 4)
                        TT(dD[:, four, :], each(ident, 4), dC[:, four, :], ALU.subtract)
                        dve.wait_ge(de_mm, 2 * LEVELS * t + half + 1)
                        TT(dE[:, four, :], each(ident, 4), quarters(6 + half), ALU.subtract).then_inc(de_ready, 1)
                    yield
                    for lv in range(1, LEVELS):
                        if lv == 1:
                            dve.wait_ge(back_copied, 12)
                            TT(heads(vn[:, t, :]), heads(vn[:, t, :]), spread(beta[:, t, :], 8), ALU.mult)
                        if lv == 2:
                            scale = k_scale[:, 0, :]
                            if t == 1:
                                link(TT(k_scale[:, 1, :], beta[:, 1, :], e_gam[:, 1, :], ALU.mult))
                                scale = k_scale[:, 1, :]
                                dve.wait_ge(s_mm, 1)
                            TT(dkb[:, :, :], heads(kn[:, t, :]), spread(scale, 8), ALU.mult).then_inc(kv_ready, 1)
                        if lv == 3 and t == 1:
                            TT(q_dec[:, :, :], q_dec[:, :, :], dqT[:, :, tok], ALU.mult).then_inc(q_scale, 1)
                        yield
                        for half in range(2):
                            four = slice(4 * half, 4 * half + 4)
                            dve.wait_ge(de_mm, 2 * (LEVELS * t + lv) + half + 1)
                            dve.wait_ge(de_ready, 2 * (LEVELS * t + lv - 1) + half + 1)
                            if lv < LEVELS - 1:
                                TT(dD[:, four, :], dD[:, four, :], quarters(de_bank(lv, half)), ALU.subtract)
                            TT(dE[:, four, :], dE[:, four, :], quarters(de_bank(lv, half) + 1),
                               ALU.subtract).then_inc(de_ready, 1)
                        yield
                    if t == 1:
                        yield
                    dve.wait_ge(u_mm, t + 1)
                    dve.tensor_copy(v_new[:, :, :], quarters(4, 2)).then_inc(vnew_ready, 1)
                    yield
                    if t == 0:
                        yield
                    dve.wait_ge(o_sq, t + 1)
                    link(dve.tensor_reduce(o_ss, dD[:, :, :], AX.X, ALU.add))
                    TS(o_ss, o_ss, 1.0 / B_HD, EPS, ALU.mult, ALU.add).then_inc(o_ms, 1)
                    dve.wait_ge(o_rs, t + 1)
                    dst = heads(qn[:, t, :])
                    link(TT(dst, quarters(4, 2), spread(o_r, 8), ALU.mult))
                    link(TT(dst, dst, each(onorm, 8), ALU.mult))
                    dve.wait_ge(evac_act, by["z"][1].n_act)
                    TT(dst, dst, heads(zs[:, t, :]), ALU.mult).then_inc(o_done, 1)
                    yield
                for _ in range(4):
                    yield
                turned_low(8, 0)

            def turned_low(kt, first):
                for m in range(4):
                    dve.wait_ge(turned_hi, even_resid[0].mix_h0 + first + m + 1)
                    at = slice(kt + 2 * m, kt + 2 * m + 2)
                    TT(fl[:, at, :], halves(4 + m % 2), fh[:, at, :].bitcast(F32), ALU.subtract).then_inc(pt_read, 1)

            def attention():
                for _ in range(4):
                    yield
                for s in range(len(UNITS) + 2):
                    if s < len(UNITS):
                        t, h0, n = UNITS[s]
                        dve.wait_ge(scored, s + 1)
                        if s >= 2:
                            dve.wait_ge(p_turned, s - 1)
                        dst = e_s[:, s % 2, :].rearrange("p (i c) -> p i c", i=n)
                        src = ps[:, 4 + s % 2, :].rearrange("p (i c) -> p i c", i=n)
                        mask = m_causal if t == 0 else m_window
                        link(STT(dst, src, A_HD ** -0.5, each(mask, n), ALU.mult, ALU.add))
                        nm, es = e_nm[:, s % 2, 0:n], e_es[:, s % 3, 0:n]
                        link(dve.tensor_reduce(nm, dst, AX.X, ALU.max, negate=True))
                        link(TT(nm, nm, n_sinks[:, h0:h0 + n], ALU.min))
                        TT(es, nm, sinks[:, h0:h0 + n], ALU.add).then_inc(a_nm, 1)
                    if s >= 2:
                        v = s - 2
                        t, h0, n = UNITS[v]
                        if v:
                            dve.wait_ge(a_out, v)
                        dve.wait_ge(a_exp_done, v + 1)
                        link(TT(e_rd[:, 0:n], e_sm[:, v % 3, 0:n], e_es[:, v % 3, 0:n], ALU.add))
                        link(dve.reciprocal(e_rd[:, 0:n], e_rd[:, 0:n]))
                        dve.wait_ge(pv_done, v + 1)
                        dst = att[:, t, 64 * h0:64 * (h0 + n)].rearrange("p (i d) -> p i d", i=n)
                        src = ps[:, 7, 0:64 * n].rearrange("p (i d) -> p i d", i=n)
                        TT(dst, src, spread(e_rd[:, 0:n], n, 64), ALU.mult).then_inc(a_out, 1)
                    yield
                    yield
                turned_low(0, 4)

            run_blocks(dve, stream, delta, attention, 4)
            after(blocks[-1], 3, None)
            dve.wait_ge(r_stat, 8)
            link(dve.tensor_reduce(v_mu, v_sum[:, :, :], AX.X, ALU.add))
            link(TS(v_mu, v_mu, 1.0 / D, None, ALU.mult))
            TS(v_nmu, v_mu, -1.0, None, ALU.mult).then_inc(r_stat, 1)
            dve.wait_ge(ln2_loaded, 32)
            for t in range(NT):
                link(STT(fin[:, t, :], h[:, t, :], v_mu[:, t:t + 1], ln2_g_row[:, :], ALU.subtract, ALU.mult))
            dve.wait_ge(r_sq, 2)
            TS(v_var, v_var, 1.0 / D, LN2_EPS, ALU.mult, ALU.add).then_inc(r_ms, 1)
            dve.wait_ge(r_rs, 1)
            for n in range(4):
                t, c = n // 2, slice(1024 * (n % 2), 1024 * (n % 2 + 1))
                STT(fin[:, t, c], fin[:, t, c], v_rstd[:, t:t + 1], ln2_b_row[:, c], ALU.mult,
                    ALU.add).then_inc(fin_ready, 1)

        @block.gpsimd
        def _(gp):
            gp.memset(neg_half, -0.5).then_inc(pool_init, 1)
            gp.wait_ge(pool_init, 1)

            def inverse_root(dst, src, n, wait, value, done):
                gp.wait_ge(wait, value)
                gp.tensor_tensor(dst, src, neg_half[:, 0:n], ALU.pow).then_inc(done, 1)

            inverse_root(rstd[:, 0, :], ms, 2, ms_ready, 1, rstd_ready)
            gp.wait_ge(l2_ms, 5)
            flat = "p x t h -> p (x t h)"
            gp.tensor_tensor(l2_r.rearrange(flat), l2_ss.rearrange(flat), neg_half, ALU.pow).then_inc(l2_rs, 1)
            gp.wait_ge(l2_rs, 1)
            gp.tensor_scalar(l2_q_r, l2_r[:, 0, :, :], B_HD ** -0.5, None, ALU.mult).then_inc(l2_rs, 1)
            gp.wait_ge(l2_rs, 2)
            for t in range(NT):
                q = qn[:, t, :].rearrange("p (h c) -> p h c", h=8)
                gp.tensor_tensor(q, q, l2_q_r[:, t, :].unsqueeze(2).to_broadcast([P, 8, P]), ALU.mult).then_inc(l2_q, 1)
            for t in range(NT):
                for lv in range(LEVELS):
                    if lv == 0:
                        gp.wait_ge(masks_loaded, 16)
                        gp.wait_ge(lqk_ready, 2 * t + 1)
                        gp.wait_ge(dec_exp, 2 * t + 2)
                    elif lv == 1:
                        gp.wait_ge(de_ready, 2 * LEVELS * t + 2)
                    else:
                        gp.wait_ge(y_mm, 2 * ((LEVELS - 1) * t + lv - 1))
                    gp.tensor_tensor(dC[:, :, :], dL[:, :, :], masks[:, lv, :].unsqueeze(1).to_broadcast([P, 8, P]),
                                     ALU.mult).then_inc(c_ready, 1)
                inverse_root(o_r, o_ss, 8, o_ms, t + 1, o_rs)
            inverse_root(rstd[:, 1, :], ms, 2, ms_ready, 2, rstd_ready)
            inverse_root(rstd[:, 2, :], ms, 2, ms_ready, 3, rstd_ready)
            inverse_root(v_rstd, v_var, 2, v_ms, 1, v_rs)
            inverse_root(rstd[:, 3, :], ms, 2, ms_ready, 4, rstd_ready)
            inverse_root(rstd[:, 4, :], ms, 2, ms_ready, 5, rstd_ready)
            inverse_root(v_rstd, v_var, 2, r_ms, 1, r_rs)


_INS = ["x", "even_norm", "even_w_in", "even_conv", "even_a_log", "even_dt_bias", "even_sinks", "even_onorm",
        "even_w_out", "odd_norm", "odd_w_in", "odd_ln_g", "odd_ln_b", "odd_w_s", "odd_b_s", "odd_w_out", "ffn_norm",
        "ffn_w_gate", "ffn_w_up", "ffn_w_down", "final_norm", "w_in_2", "b_f_2", "conv_w_2", "pool_w_2",
        "pool_scale_2", "w_out_2", "ln_g_2", "ln_b_2"]


def kernel(**inputs):
    import numpy as _np
    import concourse.bacc as _bacc
    from concourse import mybir as _mybir
    from concourse.bass_utils import run_bass_kernel_spmd as _run

    nc = _bacc.Bacc("TRN2", target_bir_lowering=False, num_devices=1)
    arrays, aps = {}, {}
    squeeze = ("even_w_in", "even_w_out", "odd_w_in", "odd_w_out", "w_in_2", "w_out_2")
    for name in _INS:
        v = _np.ascontiguousarray(inputs[name])
        arrays[f"in_{name}"] = v[0] if name in squeeze else v
    arrays["in_consts"], arrays["in_pool_consts"] = shape_constants()
    for key, v in arrays.items():
        aps[key[3:]] = nc.dram_tensor(key, v.shape, _mybir.dt.from_np(v.dtype), kind="ExternalInput").ap()
    out = nc.dram_tensor("out_0", (1, SEQ, D), _mybir.dt.float32, kind="ExternalOutput").ap()
    program(nc, aps, out)
    return _run(nc, [arrays], core_ids=[0]).results[0]["out_0"]
```
